# Optimizing a Trainium2 kernel written in Bass

```python
import math
import jax, jax.numpy as jnp
from jax import lax
import numpy as np

D_MODEL = 1024
BATCH = 1
SEQ = 256
DEPTH = 2
DEC_BATCH = 8
DEC_SEQ = 1
PAST_LEN = 2048
PAGE_SIZE = 128

D_MIX = D_MODEL
HEAD_DIM = 64
SSD_WIDTH = D_MIX // 2
SSD_HEADS = SSD_WIDTH // HEAD_DIM
SSD_GROUPS = 2
SSD_STATE = 128
SSD_CONV = 4
SSD_CONV_DIM = SSD_WIDTH + 2 * SSD_GROUPS * SSD_STATE
GLA_WIDTH = D_MIX // 4
GLA_HEADS = GLA_WIDTH // HEAD_DIM
GLA_DK = HEAD_DIM // 2
GLA_QK = GLA_HEADS * GLA_DK
GLA_RANK = 16
GLA_TAU = 16.0
RET_WIDTH = D_MIX - SSD_WIDTH - GLA_WIDTH
RET_HEADS = RET_WIDTH // HEAD_DIM
ROPE_BASE = 10000.0
MEM_LEN = 256
XATTN_HEADS = 4
XATTN_HEAD_DIM = D_MODEL // XATTN_HEADS
FFN_HIDDEN = 2816
CHUNK = 128
EPS = 1e-6
IN_SIZES = (SSD_WIDTH, SSD_CONV_DIM, SSD_HEADS, GLA_QK, GLA_QK, GLA_WIDTH, GLA_WIDTH, GLA_RANK, RET_WIDTH, RET_WIDTH, RET_WIDTH, RET_WIDTH)
D_IN = sum(IN_SIZES)

kernel_name = 'hybrid_ssd_gla_ret_macaron_step'

def rmsnorm(x, w):
    xf = x.astype(jnp.float32)
    y = xf * lax.rsqrt(jnp.mean(xf * xf, axis=-1, keepdims=True) + EPS)
    return (y * w.astype(jnp.float32)).astype(x.dtype)

def split_cols(t, sizes):
    offs, acc = [], 0
    for s in sizes[:-1]:
        acc += s
        offs.append(acc)
    return jnp.split(t, offs, axis=-1)

def swiglu(x, w_up, w_down):
    gate, up = jnp.split(x @ w_up, 2, axis=-1)
    return (jax.nn.silu(gate) * up) @ w_down

def causal_dwconv(u, buf, w, b):
    full = jnp.concatenate([buf.astype(u.dtype), u], axis=1)
    out = lax.conv_general_dilated(full, w[:, None, :].astype(u.dtype), window_strides=(1,), padding='VALID',
                                   dimension_numbers=('NWC', 'WIO', 'NWC'), feature_group_count=u.shape[-1])
    return jax.nn.silu(out + b), full[:, full.shape[1] - (SSD_CONV - 1):]

def _to_chunks(t, n, c):
    return jnp.moveaxis(t.reshape((t.shape[0], n, c) + t.shape[2:]), 1, 0)

def _from_chunks(t):
    n, b, c = t.shape[:3]
    return jnp.moveaxis(t, 0, 1).reshape((b, n * c) + t.shape[3:])

def chunk_scan_scalar(q, k, v, log_a, s0):
    L = q.shape[1]
    c = math.gcd(L, CHUNK)
    n = L // c
    mask = jnp.tril(jnp.ones((c, c), dtype=bool))[None, :, :, None]

    def step(s, inp):
        qc, kc, vc, ac = (t.astype(jnp.float32) for t in inp)
        b = jnp.cumsum(ac, axis=1)
        decay = jnp.exp(jnp.where(mask, b[:, :, None, :] - b[:, None, :, :], -jnp.inf))
        scores = jnp.einsum('bthk,bshk->btsh', qc, kc) * decay
        o = jnp.einsum('btsh,bshv->bthv', scores, vc) + jnp.einsum('bthk,bhkv->bthv', qc, s) * jnp.exp(b)[..., None]
        tail = jnp.exp(b[:, -1:] - b)
        s = s * jnp.exp(b[:, -1])[:, :, None, None] + jnp.einsum('bshk,bshv->bhkv', kc * tail[..., None], vc)
        return s, o

    s_fin, o = lax.scan(step, s0.astype(jnp.float32), tuple(_to_chunks(t, n, c) for t in (q, k, v, log_a)))
    return _from_chunks(o).astype(v.dtype), s_fin.astype(s0.dtype)

def chunk_scan_vector(q, k, v, log_a, s0):
    L = q.shape[1]
    c = math.gcd(L, CHUNK)
    n = L // c
    mask = jnp.tril(jnp.ones((c, c), dtype=bool))[None, :, :, None, None]

    def step(s, inp):
        qc, kc, vc, ac = (t.astype(jnp.float32) for t in inp)
        b = jnp.cumsum(ac, axis=1)
        decay = jnp.exp(jnp.where(mask, b[:, :, None] - b[:, None], -jnp.inf))
        scores = jnp.einsum('bthk,bshk,btshk->btsh', qc, kc, decay)
        o = jnp.einsum('btsh,bshv->bthv', scores, vc) + jnp.einsum('bthk,bhkv->bthv', qc * jnp.exp(b), s)
        s = s * jnp.exp(b[:, -1])[..., None] + jnp.einsum('bshk,bshv->bhkv', kc * jnp.exp(b[:, -1:] - b), vc)
        return s, o

    s_fin, o = lax.scan(step, s0.astype(jnp.float32), tuple(_to_chunks(t, n, c) for t in (q, k, v, log_a)))
    return _from_chunks(o).astype(v.dtype), s_fin.astype(s0.dtype)

def rotary(x, pos):
    half = x.shape[-1] // 2
    inv = ROPE_BASE ** (-jnp.arange(half, dtype=jnp.float32) / half)
    ang = pos.astype(jnp.float32)[:, None] * inv[None, :]
    cos = jnp.cos(ang)[None, :, None, :]
    sin = jnp.sin(ang)[None, :, None, :]
    xf = x.astype(jnp.float32)
    x1, x2 = xf[..., :half], xf[..., half:]
    return jnp.concatenate([x1 * cos - x2 * sin, x1 * sin + x2 * cos], axis=-1)

def head_rmsnorm(o, w):
    of = o.astype(jnp.float32)
    y = of * lax.rsqrt(jnp.mean(of * of, axis=-1, keepdims=True) + EPS)
    return y.reshape(o.shape[:2] + (-1,)) * w.astype(jnp.float32)

def head_groupnorm(o, w):
    of = o.astype(jnp.float32)
    mu = jnp.mean(of, axis=-1, keepdims=True)
    d = of - mu
    y = d * lax.rsqrt(jnp.mean(d * d, axis=-1, keepdims=True) + EPS)
    return y.reshape(o.shape[:2] + (-1,)) * w.astype(jnp.float32)

def token_mix(h, pos, state, w_in, conv_w, conv_b, dt_bias, a_log, d_skip, ssd_norm_w,
              gla_w_gate, gla_b_gate, gla_norm_w, ret_norm_w, w_out):
    s_ssd, conv_buf, s_gla, s_ret = state
    bsz, L, _ = h.shape
    z, xbc, dt_raw, gq, gk, gv, gg, glr, rq, rk, rv, rg = split_cols(h @ w_in, IN_SIZES)
    xbc, conv_new = causal_dwconv(xbc, conv_buf, conv_w, conv_b)
    xs, bm, cm = split_cols(xbc, (SSD_WIDTH, SSD_GROUPS * SSD_STATE, SSD_GROUPS * SSD_STATE))
    xs = xs.reshape(bsz, L, SSD_HEADS, HEAD_DIM)
    rep = SSD_HEADS // SSD_GROUPS
    bm = jnp.repeat(bm.reshape(bsz, L, SSD_GROUPS, SSD_STATE), rep, axis=2)
    cm = jnp.repeat(cm.reshape(bsz, L, SSD_GROUPS, SSD_STATE), rep, axis=2)
    dt = jax.nn.softplus(dt_raw.astype(jnp.float32) + dt_bias.astype(jnp.float32))
    a = -jnp.exp(a_log.astype(jnp.float32))
    y_ssd, s_ssd_new = chunk_scan_scalar(cm, bm * dt[..., None], xs, dt * a, s_ssd)
    y_ssd = (y_ssd + xs * d_skip[:, None]).reshape(bsz, L, SSD_WIDTH)
    g = (y_ssd.astype(jnp.float32) * jax.nn.silu(z.astype(jnp.float32))).reshape(bsz, L, SSD_GROUPS, -1)
    y_ssd = (g * lax.rsqrt(jnp.mean(g * g, axis=-1, keepdims=True) + EPS)).reshape(bsz, L, SSD_WIDTH) * ssd_norm_w
    gq = gq.reshape(bsz, L, GLA_HEADS, GLA_DK) * GLA_DK ** -0.5
    gk = gk.reshape(bsz, L, GLA_HEADS, GLA_DK)
    gv = gv.reshape(bsz, L, GLA_HEADS, HEAD_DIM)
    log_alpha = jax.nn.log_sigmoid((glr @ gla_w_gate + gla_b_gate).astype(jnp.float32)) / GLA_TAU
    log_alpha = log_alpha.reshape(bsz, L, GLA_HEADS, GLA_DK)
    o_gla, s_gla_new = chunk_scan_vector(gq, gk, gv, log_alpha, s_gla)
    y_gla = head_rmsnorm(o_gla, gla_norm_w) * jax.nn.silu(gg.astype(jnp.float32))
    rq = rotary(rq.reshape(bsz, L, RET_HEADS, HEAD_DIM), pos)
    rk = rotary(rk.reshape(bsz, L, RET_HEADS, HEAD_DIM), pos) * HEAD_DIM ** -0.5
    rv = rv.reshape(bsz, L, RET_HEADS, HEAD_DIM)
    log_gamma = jnp.log1p(-jnp.exp2(-5.0 - jnp.arange(RET_HEADS, dtype=jnp.float32)))
    o_ret, s_ret_new = chunk_scan_scalar(rq, rk, rv, jnp.broadcast_to(log_gamma, (bsz, L, RET_HEADS)), s_ret)
    y_ret = head_groupnorm(o_ret, ret_norm_w) * jax.nn.silu(rg.astype(jnp.float32))
    y = jnp.concatenate([y_ssd, y_gla, y_ret], axis=-1).astype(h.dtype) @ w_out
    return y, (s_ssd_new, conv_new, s_gla_new, s_ret_new)

def cross_attend(h, mem_k, mem_v, w_q, w_o):
    bsz, L, _ = h.shape
    q = (h @ w_q).reshape(bsz, L, XATTN_HEADS, XATTN_HEAD_DIM)
    s = jnp.einsum('blhd,bmhd->bhlm', q, mem_k).astype(jnp.float32) * XATTN_HEAD_DIM ** -0.5
    p = jax.nn.softmax(s, axis=-1)
    o = jnp.einsum('bhlm,bmhd->blhd', p.astype(mem_v.dtype), mem_v).reshape(bsz, L, D_MODEL)
    return o @ w_o

def decoder_layer(x, pos, mem_k, mem_v, state, lw):
    (n1, f1u, f1d, n2, w_in, cw, cb, dtb, alog, dsk, ssdw, gw, gb, glaw, retw, wo,
     n3, xq, xo, n4, f2u, f2d) = lw
    x = x + 0.5 * swiglu(rmsnorm(x, n1), f1u, f1d)
    mix, new_state = token_mix(rmsnorm(x, n2), pos, state, w_in, cw, cb, dtb, alog, dsk, ssdw, gw, gb, glaw, retw, wo)
    x = x + mix
    x = x + cross_attend(rmsnorm(x, n3), mem_k, mem_v, xq, xo)
    x = x + 0.5 * swiglu(rmsnorm(x, n4), f2u, f2d)
    return x, new_state

def setup_inputs(seed: int = 0) -> dict:
    key = jax.random.key(seed)
    k = jax.random.split(key, 40)

    def nrm(i, shape, scale=1.0):
        return jax.random.normal(k[i], shape, jnp.float32) * scale

    def gain(i, shape):
        return 1.0 + nrm(i, shape, 0.02)

    dt0 = jnp.exp(jax.random.uniform(k[33], (DEPTH, SSD_HEADS), jnp.float32, minval=math.log(1e-3), maxval=math.log(1e-1)))
    dt_bias = dt0 + jnp.log(-jnp.expm1(-dt0))
    a_log = jnp.log(jax.random.uniform(k[34], (DEPTH, SSD_HEADS), jnp.float32, minval=1.0, maxval=16.0))
    return {
        'x_prompt': nrm(0, (BATCH, SEQ, D_MODEL)),
        'x_sample': nrm(1, (DEC_BATCH, DEC_SEQ, D_MODEL)),
        'mem_prompt': nrm(2, (BATCH, MEM_LEN, D_MODEL)),
        'cache_mem_k': nrm(3, (DEPTH, DEC_BATCH, MEM_LEN, XATTN_HEADS, XATTN_HEAD_DIM)),
        'cache_mem_v': nrm(4, (DEPTH, DEC_BATCH, MEM_LEN, XATTN_HEADS, XATTN_HEAD_DIM)),
        'state_ssd': nrm(5, (DEPTH, DEC_BATCH, SSD_HEADS, SSD_STATE, HEAD_DIM), 0.1),
        'state_ssd_conv': nrm(6, (DEPTH, DEC_BATCH, SSD_CONV - 1, SSD_CONV_DIM)),
        'state_gla': nrm(7, (DEPTH, DEC_BATCH, GLA_HEADS, GLA_DK, HEAD_DIM), 0.1),
        'state_ret': nrm(8, (DEPTH, DEC_BATCH, RET_HEADS, HEAD_DIM, HEAD_DIM), 0.1),
        'norm_ffn1': gain(9, (DEPTH, D_MODEL)),
        'ffn1_w_up': nrm(10, (DEPTH, D_MODEL, 2 * FFN_HIDDEN), D_MODEL ** -0.5),
        'ffn1_w_down': nrm(11, (DEPTH, FFN_HIDDEN, D_MODEL), FFN_HIDDEN ** -0.5),
        'norm_mix': gain(12, (DEPTH, D_MODEL)),
        'w_in': nrm(13, (DEPTH, D_MODEL, D_IN), D_MODEL ** -0.5),
        'conv_w': nrm(14, (DEPTH, SSD_CONV, SSD_CONV_DIM), SSD_CONV ** -0.5),
        'conv_b': nrm(15, (DEPTH, SSD_CONV_DIM), 0.02),
        'dt_bias': dt_bias,
        'a_log': a_log,
        'd_skip': gain(16, (DEPTH, SSD_HEADS)),
        'ssd_norm_w': gain(17, (DEPTH, SSD_WIDTH)),
        'gla_w_gate': nrm(18, (DEPTH, GLA_RANK, GLA_QK), GLA_RANK ** -0.5),
        'gla_b_gate': nrm(19, (DEPTH, GLA_QK), 0.02),
        'gla_norm_w': gain(20, (DEPTH, GLA_WIDTH)),
        'ret_norm_w': gain(21, (DEPTH, RET_WIDTH)),
        'w_out': nrm(22, (DEPTH, D_MIX, D_MODEL), D_MIX ** -0.5),
        'norm_xattn': gain(23, (DEPTH, D_MODEL)),
        'xattn_w_q': nrm(24, (DEPTH, D_MODEL, D_MODEL), D_MODEL ** -0.5),
        'xattn_w_k': nrm(25, (DEPTH, D_MODEL, D_MODEL), D_MODEL ** -0.5),
        'xattn_w_v': nrm(26, (DEPTH, D_MODEL, D_MODEL), D_MODEL ** -0.5),
        'xattn_w_o': nrm(27, (DEPTH, D_MODEL, D_MODEL), D_MODEL ** -0.5),
        'norm_ffn2': gain(28, (DEPTH, D_MODEL)),
        'ffn2_w_up': nrm(29, (DEPTH, D_MODEL, 2 * FFN_HIDDEN), D_MODEL ** -0.5),
        'ffn2_w_down': nrm(30, (DEPTH, FFN_HIDDEN, D_MODEL), FFN_HIDDEN ** -0.5),
        'final_norm_w': gain(31, (D_MODEL,)),
    }

def reference(x_prompt, x_sample, mem_prompt, cache_mem_k, cache_mem_v, state_ssd, state_ssd_conv, state_gla, state_ret,
              norm_ffn1, ffn1_w_up, ffn1_w_down, norm_mix, w_in, conv_w, conv_b, dt_bias, a_log, d_skip, ssd_norm_w,
              gla_w_gate, gla_b_gate, gla_norm_w, ret_norm_w, w_out, norm_xattn, xattn_w_q, xattn_w_k, xattn_w_v,
              xattn_w_o, norm_ffn2, ffn2_w_up, ffn2_w_down, final_norm_w):
    bp, lp = x_prompt.shape[0], x_prompt.shape[1]
    ls = x_sample.shape[1]
    pos_p = jnp.arange(lp, dtype=jnp.int32)
    pos_s = PAST_LEN + jnp.arange(ls, dtype=jnp.int32)
    dtp = x_prompt.dtype
    zero_state = (jnp.zeros((bp, SSD_HEADS, SSD_STATE, HEAD_DIM), dtp),
                  jnp.zeros((bp, SSD_CONV - 1, SSD_CONV_DIM), dtp),
                  jnp.zeros((bp, GLA_HEADS, GLA_DK, HEAD_DIM), dtp),
                  jnp.zeros((bp, RET_HEADS, HEAD_DIM, HEAD_DIM), dtp))
    xp, xs = x_prompt, x_sample
    ssd_p, conv_p, gla_p, ret_p, mk_p, mv_p = [], [], [], [], [], []
    ssd_s, conv_s, gla_s, ret_s = [], [], [], []
    for l in range(DEPTH):
        lw = (norm_ffn1[l], ffn1_w_up[l], ffn1_w_down[l], norm_mix[l], w_in[l], conv_w[l], conv_b[l], dt_bias[l],
              a_log[l], d_skip[l], ssd_norm_w[l], gla_w_gate[l], gla_b_gate[l], gla_norm_w[l], ret_norm_w[l], w_out[l],
              norm_xattn[l], xattn_w_q[l], xattn_w_o[l], norm_ffn2[l], ffn2_w_up[l], ffn2_w_down[l])
        mk = (mem_prompt @ xattn_w_k[l]).reshape(bp, MEM_LEN, XATTN_HEADS, XATTN_HEAD_DIM)
        mv = (mem_prompt @ xattn_w_v[l]).reshape(bp, MEM_LEN, XATTN_HEADS, XATTN_HEAD_DIM)
        xp, (s1, c1, g1, r1) = decoder_layer(xp, pos_p, mk, mv, zero_state, lw)
        xs, (s2, c2, g2, r2) = decoder_layer(xs, pos_s, cache_mem_k[l], cache_mem_v[l],
                                             (state_ssd[l], state_ssd_conv[l], state_gla[l], state_ret[l]), lw)
        ssd_p.append(s1); conv_p.append(c1); gla_p.append(g1); ret_p.append(r1); mk_p.append(mk); mv_p.append(mv)
        ssd_s.append(s2); conv_s.append(c2); gla_s.append(g2); ret_s.append(r2)
    y_prompt = rmsnorm(xp, final_norm_w)
    y_sample = rmsnorm(xs, final_norm_w)
    return (y_prompt, y_sample,
            jnp.stack(ssd_p), jnp.stack(conv_p), jnp.stack(gla_p), jnp.stack(ret_p), jnp.stack(mk_p), jnp.stack(mv_p),
            jnp.stack(ssd_s), jnp.stack(conv_s), jnp.stack(gla_s), jnp.stack(ret_s))


_drawn_inputs = setup_inputs


def setup_inputs(seed=0):
    import zlib

    import numpy as np

    out = dict(_drawn_inputs(seed))
    spreads = {}
    factors = {'norm_ffn1': 3.044,
     'd_skip': 7.07,
     'ssd_norm_w': 3.003,
     'gla_b_gate': 6.353,
     'gla_norm_w': 5.922,
     'ret_norm_w': 8.0,
     'norm_xattn': 8.0,
     'norm_ffn2': 5.811,
     'final_norm_w': 2.896}
    for name, (base, spread) in spreads.items():
        noise = np.random.default_rng([zlib.crc32(name.encode()), seed]).standard_normal(out[name].shape)
        drawn = base * np.exp(spread * noise) if base else spread * noise
        out[name] = __import__('jax').numpy.asarray(drawn.astype(out[name].dtype))
    for name, factor in factors.items():
        out[name] = (out[name] * factor).astype(out[name].dtype)
    return out
```

```python
from contextlib import ExitStack

import numpy as np

import concourse.bass as bass
from concourse import mybir

F32 = mybir.dt.float32
F32R = mybir.dt.float32r
ALU = mybir.AluOpType
ACT = mybir.ActivationFunctionType
AX = mybir.AxisListType

P = 128
D = 1024
KB = D // P
TP, NS = 256, 8
T = TP + NS
FF = 2816
HALF = FF // P // 2
EPS = 1e-6

TILES = 8
CH = TILES * P
RAW, SPL = 11, 3
HALF_CH = 3 * HALF
K_FFN1 = 0
K_WIN = K_FFN1 + 2 * HALF_CH
N_WIN = 26
K_MEMK = K_WIN + N_WIN
K_MEMV = K_MEMK + 8
K_WOUT = K_MEMV + 8
K_Q = K_WOUT + 8
K_O = K_Q + 8
K_FFN2 = K_O + 8
NCH = K_FFN2 + 2 * HALF_CH
assert NCH % (RAW * SPL) == 0 and K_FFN2 % (RAW * SPL) == 0

HEADS_S, HEADS = 8, 4
SM = 48
PADW = TP + 3 + 4 * NS
LEVELS = [128, 64, 32, 16, 8, 4, 2, 1]

B_XBC, B_Z, B_GQ, B_GK, B_GV, B_RQ, B_RK, B_RV, B_GG = 0, 8, 12, 13, 14, 16, 18, 20, 22


def columns(*fields):
    at, where = 0, {}
    for name, width in fields:
        where[name] = (at, at + width)
        at += width
    return where, at


PAR, NPAR = columns(("n1", 8), ("n2", 8), ("n3", 8), ("n4", 8), ("cw", 32), ("cb", 8), ("ws", 8 * SM + 80),
                    ("gwg", 128), ("dtb", 1), ("alog", 1), ("dsk", 4), ("ssdw", 4), ("glaw", 2), ("retw", 2),
                    ("glab", 1))
CST, NCST = columns(("ident", 128), ("ones", 128), ("tri", 384), ("cos", T), ("sin", T), ("decay", 4 * 384),
                    ("rtail", 256), ("gamma", 1), ("lmask", 8 * 128), ("bones", 128), ("vsel", 256), ("hmask", 4),
                    ("id64", 64), ("eps", 1), ("zero", 1))


def build(nc, depth, wts, params, consts, x_in, mem_in, ck, cv, st_ssd, st_conv, st_gla, st_ret,
          y_out, o_conv, o_ssdp, o_grp, o_mk, o_mv, o_ssds, o_glas, o_rets):
    with ExitStack() as ctx:
        base = (nc.sbuf_base + 63) // 64 * 64
        room = (nc.sbuf_usable_end - base - 128) // 64 * 64
        ctx.enter_context(nc.sbuf_tensor("arena", [P, room // 4], F32))
        top = [base]
        sizes = {F32: 4, F32R: 4}

        def place(name, shape, dt=F32, at=None):
            off = top[0] if at is None else at
            n = 4 * int(np.prod(shape[1:]))
            if at is None:
                top[0] += (n + 31) // 32 * 32
            assert off + n <= base + room, (name, off + n - base - room)
            return nc.alloc_sbuf_tensor_at(name, list(shape), dt, offset=off)

        raw = place("raw", [P, RAW, CH])
        w_hi = place("w_hi", [P, SPL, CH], F32R)
        w_lo = place("w_lo", [P, SPL, CH], F32R)
        x = place("x", [P, KB, T])
        xn_at = top[0]
        xn_hi = place("xn_hi", [P, KB, T], F32R)
        xn_lo = place("xn_lo", [P, KB, T], F32R)
        h_at = top[0]
        h_hi = place("h_hi", [P, HALF, T], F32R)
        h_lo = place("h_lo", [P, HALF, T], F32R)
        mem_hi = place("mem_hi", [P, KB, TP], F32R)
        mem_lo = place("mem_lo", [P, KB, TP], F32R)
        par = place("par", [P, NPAR])
        cst = place("cst", [P, NCST])
        r_bc = place("r_bc", [P, T])
        mix_at = top[0]

        sq = place("sq", [P, KB, T])
        gbuf = place("gbuf", [P, 2, T], at=mix_at + 8448)
        ubuf = place("ubuf", [P, 2, T], at=mix_at + 8448 + 2112)
        sbuf_ = place("sbuf", [P, 2, T], at=mix_at + 8448 + 4224)
        h32 = place("h32", [P, 2, T], at=mix_at + 8448 + 6336)
        yo = place("yo", [P, KB, T], at=mix_at + 16896)
        mem_raw = place("mem_raw", [P, KB, TP], at=mix_at)

        top[0] = mix_at
        xc = place("xc", [P, 8, T])
        yg = place("yg", [P, 8, T])
        qkv = place("qkv", [P, 10, T])
        bsum = place("bsum", [8, T])
        glog = place("glog", [P, T])
        kst = place("kst", [P, 2, TP])
        vst = place("vst", [P, 2, 512])
        convst = place("convst", [P, 8, 9, 3])
        convld = place("convld", [P, 8, NS, 3])
        gst = place("gst", [P, NS, 64])
        rst = place("rst", [P, 2, NS, 64])
        tmp_at = top[0]
        cbuf = place("cbuf", [P, 2, 288], at=tmp_at)
        sm = place("sm", [SM, T], at=tmp_at + 2304)
        sp = [place(f"sp{i}", [P, T], at=tmp_at + 3360 + 1056 * i) for i in range(3)]
        xp = place("xp", [P, 8, PADW], at=h_at)
        ws_hi = place("ws_hi", [P, 8 * SM + 80], F32R, at=h_at + 9344)
        ws_lo = place("ws_lo", [P, 8 * SM + 80], F32R, at=h_at + 9344 + 1856)
        dt8 = place("dt8", [8, T], at=h_at + 13056)
        na8 = place("na8", [8, 1], at=h_at + 14112)
        la8 = place("la8", [8, T], at=h_at + 14144)
        e8 = place("e8", [8, T], at=h_at + 19456)
        rp = [place(f"rp{i}", [P, 2, T], at=h_at + 15232 + 2112 * i) for i in range(2)]
        bs = place("bs", [P, 2, 8])
        dec = place("dec", [P, 8, NS])
        xdt = place("xdt", [P, 4, T])
        gm = place("gm", [P, 2, 384])
        dbuf = place("dbuf", [P, 2, 392])
        xtok = place("xtok", [P, 2, 512], at=h_at)
        btok = place("btok", [P, 2, 256], at=h_at + 4096)
        xtail = place("xtail", [P, 2, 512], at=h_at + 6144)
        mbuf = place("mbuf", [P, 2, 384], at=h_at + 10240)
        xe = place("xe", [P, NS, P], at=h_at + 13312)
        tb = place("tb", [P, NS, P], at=h_at)
        ssdo = place("ssdo", [P, 512], at=h_at + 21184)
        sst = place("sst", [P, 4, NS, P], at=xn_at)
        ke = place("ke", [P, 9, TP], at=h_at)
        qe = place("qe", [P, 8, TP], at=h_at + 9216)
        gvtok = place("gvtok", [P, 2, TP], at=h_at + 17408)
        rvtok = place("rvtok", [P, 2, TP], at=h_at + 19456)
        gktok = place("gktok", [P, 2, P], at=h_at + 21504)
        mg = place("mg", [P, 2, 384], at=tmp_at)
        gtmp = place("gtmp", [P, 512], at=tmp_at + 3072)
        rktok = place("rktok", [P, 2, 2, P], at=tmp_at + 5120)
        sto = place("sto", [P, 3, 64], at=tmp_at + 7168)
        gdec = place("gdec", [P, NS], at=tmp_at + 7936)
        qx = place("qx", [P, 3, NS, 4], at=tmp_at + 7968)
        yb = place("yb", [P, 4, T], at=tmp_at + 8352)
        xg = place("xg", [P, 2, NS, 64], at=h_at)
        tg = place("tg", [P, NS, 64], at=h_at + 4096)
        sq4 = place("sq4", [P, 4, T], at=h_at + 6144)
        rn = place("rn", [P, 4, T], at=h_at + 10368)
        qt = place("qt", [P, KB, T], at=mix_at)
        kt = place("kt", [P, KB, TP], at=mix_at + 8448)
        vt = place("vt", [P, 2, D], at=mix_at + 16640)
        pr = place("pr", [P, 2, 2, TP], at=mix_at + 24832)
        prt = place("prt", [P, 2, 2, TP], at=mix_at + 28928)
        mx = place("mx", [P, 4, 2], at=mix_at + 33024)
        nmx = place("nmx", [P, 4, 2], at=mix_at + 33056)
        psm = place("psm", [P, 4, 2], at=mix_at + 33088)
        rsm = place("rsm", [P, 4, 2], at=mix_at + 33120)
        ps_s = place("ps_s", [32, TP], at=mix_at + 33408)
        m32 = place("m32", [32, 4], at=mix_at + 34688)
        KV_AT = [h_at, h_at + 8192, mix_at + 34720, mix_at + 42912]
        kv = [place(f"kv{i}", [P, 2048], at=KV_AT[i]) for i in range(4)]
        apart = [place(f"apart{i}", [P, 33 * 32], at=(h_at + 16384, mix_at + 51104)[i]) for i in range(2)]
        os_s = place("os_s", [32, TP], at=mix_at + 55328)

        bank = [ctx.enter_context(nc.psum_tensor(f"bank{i}", [P, 512], F32)) for i in range(8)]

        def pc(name, a=0, b=None, rows=slice(0, P)):
            lo, hi = PAR[name]
            return par[rows, lo + a:hi if b is None else lo + b]

        def cc(name, a=0, b=None, rows=slice(0, P)):
            lo, hi = CST[name]
            return cst[rows, lo + a:hi if b is None else lo + b]

        ident = cc("ident")
        ones = cc("ones")

        def new(name):
            return ctx.enter_context(nc.semaphore(name))

        loaded = new("loaded")
        mem_split = new("mem_split")
        par_landed = new("par_landed")
        landed = [new(f"landed{i}") for i in range(RAW)]
        hi_ready = new("hi_ready")
        lo_ready = new("lo_ready")
        layer_done = new("layer_done")
        go = {n: new(f"go_{n}") for n in ("pe", "act", "dve", "pool")}

        names = """chunk_used xn_hi xn_lo sq_ready ss_ready r_ready x_done g_ready up_evac s_ready h32_ready hhi_ready h_ready
            down_done st_in st_ssd_in win_evac ws_hi_ready ws_ready small_done small_evac gate_done conv_done xs_ready
            conv_out_ready z_ready gg_ready bsum_ready lp_act lp_dve bs_done bs_ready dtb_done xdt_ready btok_done
            btok_ready xtok_done xtok_ready g_done gm_ready bc_done d_ready e_ready m_ready y_done y_evac ssdp_done
            ssdp_ready xe_ready xb_done xb_evac sst_ready o_done ssd_gated ssd_sq sg_done sg_r vt_done vt_ready d9_ready
            e9_ready ke_ready gkt_done gkt_ready rkt_ready rkt_done rktok_ready lv_done lv_evac mg_ready gy_done gy_evac
            gs_done gs_ready rsc_done mr_ready ry_done ry_evac rs_done xg_ready vb_done gdec_ready gst_ready qx_ready
            go_done gsq_ready gms_done gms_r mu_done mk_ready mk_out0 mk_out1 mv_ready mv_out0 mv_out1 y_hi y_lo ssdp_out
            ssds_out q_ready kv_in0 kv_in1 kv_in2 kv_in3 kv_used sc_done mx_ready p_ready pn_ready pt_done prt_ready
            pv_done o_hi o_lo ss_zero ss_q ss_mx ss_p ss_pn ss_t2 ss_pts ss_o ss_t3 act_chain dve_chain mix_out y_final
            ktv_in""".split()
        sem = {n: new(n) for n in names}
        first, last = sem[names[0]].num, sem[names[-1]].num
        assert last - first == len(names) - 1

        block = ctx.enter_context(nc.Block())

        X_DONE = [0, 16, 24, 32]

        vg, ng, eg, ug = sp[1], sp[2], rp[0][:, 0, :], rp[1][:, 0, :]

        SUMS = [bank[6], bank[3], bank[6], bank[6]]

        def layer_end(eng, name):
            eng.drain().then_inc(layer_done, 1)
            eng.wait_ge(go[name], 1)
            eng.sem_inc(go[name], -1)

        @block.sync
        def _(sp):
            sp.dma_start(cst[:], consts).then_inc(loaded, 16)
            sp.dma_start(par[:], params[0]).then_inc(loaded, 16)
            sp.dma_start(x[:], x_in).then_inc(loaded, 16)
            sp.dma_start(mem_raw[:], mem_in).then_inc(loaded, 16)
            for s in range(RAW):
                sp.dma_start(raw[:, s, :], wts[s]).then_inc(landed[s], 16)

            with sp.Fori(0, depth) as layer:
                def at_layer(t):
                    return t[bass.ds(layer, 1)]

                def row(t, k):
                    return t[bass.ds(layer * NCH + (k + RAW), 1)].rearrange("a p c -> (a p) c")

                def stream(k):
                    sp.wait_ge(lo_ready, k + 1)
                    sp.dma_start(raw[:, k % RAW, :], row(wts, k)).then_inc(landed[k % RAW], 16)

                def stream_loop(g0, g1):
                    with sp.Fori(g0, g1) as g:
                        for s in range(RAW):
                            sp.wait_ge(lo_ready, g * RAW + (s + 1))
                            sp.dma_start(raw[:, s, :], row(wts, g * RAW + s)).then_inc(landed[s], 16)

                def load(dst, src, name):
                    sp.dma_start(dst, src).then_inc(sem[name], 16)

                def store(dst, src, name):
                    sp.dma_start(dst, src).then_inc(sem[name], 16)

                load(convld[:].rearrange("p a b c -> p (a b c)"), at_layer(st_conv).rearrange("a p c -> (a p) c"), "st_in")
                load(gst[:].rearrange("p a b -> p (a b)"), at_layer(st_gla).rearrange("a p c -> (a p) c"), "st_in")
                load(rst[:].rearrange("p a b c -> p (a b c)"), at_layer(st_ret).rearrange("a p c -> (a p) c"), "st_in")
                stream_loop(0, K_MEMK // RAW)
                for k in range(K_MEMK // RAW * RAW, K_FFN2):
                    stream(k)
                    if k == K_MEMK + 3:
                        sp.wait_ge(sem["chunk_used"], K_MEMK)
                        load(sst[:].rearrange("p a b c -> p (a b c)"), at_layer(st_ssd).rearrange("a p c -> (a p) c"), "st_ssd_in")
                        sp.wait_ge(sem["conv_out_ready"], 2)
                        store(at_layer(o_conv).rearrange("a p c -> (a p) c"), convst[:].rearrange("p a b c -> p (a b c)"), "mix_out")
                    if K_MEMK + 3 <= k < K_MEMK + 11:
                        m = k - K_MEMK - 3
                        sp.wait_ge(sem["mk_ready"], m + 1)
                        store(o_mk[bass.ds(layer * KB + m, 1)].rearrange("a p c -> (a p) c"), kst[:, m % 2, :], f"mk_out{m % 2}")
                    if k in (K_MEMV + 6, K_MEMV + 10):
                        half = (k - K_MEMV - 6) // 4
                        sp.wait_ge(sem["mv_ready"], 2 * (half + 1))
                        store(at_layer(o_mv).rearrange("a p m c -> (a p) m c")[:, :, 512 * half:512 * half + 512], vst[:], f"mv_out{half}")
                    if k == K_MEMV:
                        sp.wait_ge(sem["ssdp_ready"], 1)
                        store(at_layer(o_ssdp).rearrange("a p c -> (a p) c"), ssdo[:], "ssdp_out")
                    if k == K_MEMV + 6:
                        sp.wait_ge(sem["sst_ready"], 4)
                        store(at_layer(o_ssds).rearrange("a p c -> (a p) c"), sst[:].rearrange("p a b c -> p (a b c)"), "ssds_out")
                    if k == K_WOUT + 3:
                        sp.wait_ge(sem["gs_ready"], 12)
                        store(at_layer(o_grp).rearrange("a p c -> (a p) c"), sto[:].rearrange("p a b -> p (a b)"), "mix_out")
                        sp.wait_ge(sem["gst_ready"], 1)
                        store(at_layer(o_glas).rearrange("a p c -> (a p) c"), gst[:].rearrange("p a b -> p (a b)"), "mix_out")
                        sp.wait_ge(sem["gst_ready"], 3)
                        store(at_layer(o_rets).rearrange("a p c -> (a p) c"), rst[:].rearrange("p a b c -> p (a b c)"), "mix_out")
                        sp.wait_ge(sem["y_lo"], 8)
                        sp.wait_ge(sem["mix_out"], 64)
                        for i in range(2):
                            sp.wait_ge(sem[f"mk_out{i}"], 64)
                            sp.wait_ge(sem[f"mv_out{i}"], 16)
                        load(kt[:], o_mk[bass.ds(layer * KB, KB)].rearrange("a p c -> p a c"), "ktv_in")
                        load(vt[:], at_layer(o_mv).rearrange("a p m c -> (a p) m c"), "ktv_in")
                        for n in range(4):
                            load(kv[n][:], ck[bass.ds(layer * NS + n, 1)].rearrange("a p c -> (a p) c"), f"kv_in{n}")
                    if k == K_Q + 4:
                        for n in range(4, 2 * NS):
                            sp.wait_ge(sem["kv_used"], n - 3)
                            src = ck if n < NS else cv
                            load(kv[n % 4][:], src[bass.ds(layer * NS + n % NS, 1)].rearrange("a p c -> (a p) c"), f"kv_in{n % 4}")
                stream_loop(K_FFN2 // RAW, K_FFN2 // RAW + 1)
                sp.wait_ge(sem["xn_lo"], 4 * KB)
                sp.dma_start(par[:], params[bass.ds(layer + 1, 1)].rearrange("a p c -> (a p) c")).then_inc(par_landed, 16)
                stream_loop(K_FFN2 // RAW + 1, NCH // RAW)
                sp.wait_ge(sem["ssdp_out"], 16)
                sp.wait_ge(sem["ssds_out"], 16)
                sp.wait_ge(par_landed, 16)
                sp.sem_inc(par_landed, -16)
                sp.wait_ge(layer_done, 4)
                sp.sem_clear(range(first, last + 1))
                sp.sem_inc(layer_done, -4)
                sp.sem_inc(hi_ready, -NCH)
                sp.sem_inc(lo_ready, -NCH)
                for n in go:
                    sp.sem_inc(go[n], 1)

            for s in range(SPL, RAW):
                sp.wait_ge(landed[s], 16)
            sp.wait_ge(sem["h_ready"], KB)
            sp.dma_start(y_out, yo[:]).then_inc(sem["mix_out"], 16)
            sp.wait_ge(sem["mix_out"], 16)

        @block.gpsimd
        def _(pool):
            def low_part(k, wait):
                pool.wait_ge(hi_ready, wait)
                pool.tensor_tensor(w_lo[:, k % SPL, :], raw[:, k % RAW, :], w_hi[:, k % SPL, :].bitcast(F32),
                                   ALU.subtract).then_inc(lo_ready, 1)

            for k in range(SPL):
                low_part(k, k + 1)
            with pool.Fori(0, depth):
                with pool.Fori(0, NCH // (RAW * SPL)) as g:
                    for j in range(RAW * SPL):
                        low_part(j + SPL, g * (RAW * SPL) + (j + SPL + 1))
                layer_end(pool, "pool")

        @block.scalar
        def _(act):
            chain = [0]

            def link(ins):
                chain[0] += 1
                ins.then_inc(sem["act_chain"], 1)
                act.wait_ge(sem["act_chain"], chain[0])

            def high_part(k, used=None):
                if used is not None:
                    act.wait_ge(sem["chunk_used"], used)
                act.wait_ge(landed[k % RAW], 16)
                act.sem_inc(landed[k % RAW], -16)
                act.activation(w_hi[:, k % SPL, :], raw[:, k % RAW, :], ACT.Copy).then_inc(hi_ready, 1)

            def ahead(k):
                high_part(k + SPL, k + 1)

            def norm_parts(n, x_known=True):
                if n in (2, 3):
                    act.wait_ge(sem["chunk_used"], (K_Q, K_FFN2)[n - 2])
                for b in range(KB):
                    if x_known and n > 0:
                        act.wait_ge(sem["x_done"], X_DONE[n] - KB + b + 1)
                    act.activation(xn_hi[:, b, :], x[:, b, :], ACT.Copy, scale=pc(f"n{n + 1}", b, b + 1)).then_inc(sem["xn_hi"], 1)
                    act.activation(sq[:, b, :], x[:, b, :], ACT.Square).then_inc(sem["sq_ready"], 1)

            def norm_scale(n):
                act.wait_ge(sem["ss_ready"], n + 1)
                link(act.activation(r_bc[:], SUMS[n][:, 0:T], ACT.Ln, scale=1.0 / D, bias=cc("eps")))
                act.activation(r_bc[:], r_bc[:], ACT.Exp, scale=-0.5).then_inc(sem["r_ready"], 1)

            def ffn(f):
                k0 = (K_FFN1, K_FFN2)[f]
                norm_parts((0, 3)[f])
                norm_scale((0, 3)[f])
                with act.Fori(0, 2) as half:
                    k = half * HALF_CH + k0
                    b = half * HALF + 2 * HALF * f
                    for j in range(HALF):
                        high_part(2 * j + SPL, k + (2 * j + 1))
                        act.wait_ge(sem["g_ready"], b + (j + 1))
                        act.activation(sbuf_[:, j % 2, :], gbuf[:, j % 2, :], ACT.Silu).then_inc(sem["s_ready"], 1)
                        high_part(2 * j + 1 + SPL, k + (2 * j + 2))
                        act.wait_ge(sem["h32_ready"], b + (j + 1))
                        act.activation(h_hi[:, j, :], h32[:, j % 2, :], ACT.Copy).then_inc(sem["hhi_ready"], 1)
                    for c in range(2 * HALF, HALF_CH):
                        high_part(c + SPL, k + (c + 1))

            act.wait_ge(loaded, 64)
            act.activation(mem_hi[:], mem_raw[:], ACT.Copy).then_inc(mem_split, 1)
            act.wait_ge(mem_split, 2)
            for k in range(SPL):
                high_part(k)
            with act.Fori(0, depth):
                chain[0] = 0
                ffn(0)

                norm_parts(1)
                act.activation(ws_hi[:], pc("ws"), ACT.Copy).then_inc(sem["ws_hi_ready"], 1)
                norm_scale(1)
                act.activation(na8[:], pc("alog", rows=slice(0, 8)), ACT.Exp).then_inc(sem["z_ready"], 1)

                def conv_act(n):
                    act.wait_ge(sem["conv_done"], n + 1)
                    act.activation(xc[:, n, 0:TP], cbuf[:, n % 2, 0:TP], ACT.Silu)
                    act.activation(xc[:, n, TP:T], cbuf[:, n % 2, TP + 3:TP + 3 + 29:4], ACT.Silu).then_inc(sem["xs_ready"], 1)

                for n in range(N_WIN):
                    ahead(K_WIN + n)
                    if 1 <= n <= 8:
                        conv_act(n - 1)
                    if n == 12:
                        act.wait_ge(sem["win_evac"], 12)
                        act.activation(yg[:, 0:4, :], yg[:, 0:4, :], ACT.Silu).then_inc(sem["z_ready"], 1)
                    if n == 14:
                        act.wait_ge(sem["lp_dve"], 1)
                        act.activation(e8[:], sp[0][0:8, :], ACT.Exp).then_inc(sem["lp_act"], 1)
                        act.wait_ge(sem["lp_dve"], 2)
                        act.activation(eg, ng[:], ACT.Exp).then_inc(sem["lp_act"], 1)
                    if n == 16:
                        act.wait_ge(sem["lp_dve"], 3)
                        act.activation(e8[:], dt8[:], ACT.Ln).then_inc(sem["lp_act"], 1)
                        act.wait_ge(sem["lp_dve"], 4)
                        act.activation(eg, ug, ACT.Ln).then_inc(sem["lp_act"], 1)
                act.wait_ge(sem["win_evac"], N_WIN)
                act.activation(yg[:, 4:8, :], yg[:, 4:8, :], ACT.Silu).then_inc(sem["gg_ready"], 1)

                def fill(k):
                    ahead(k)
                    if k < K_MEMV:
                        m = k - K_MEMK
                        if m >= 2:
                            act.wait_ge(sem[f"mk_out{m % 2}"], 16 * (m // 2))
                        act.activation(kst[:, m % 2, :], bank[m % 4][:, 0:TP], ACT.Copy).then_inc(sem["mk_ready"], 1)
                    elif (k - K_MEMV) % 4 == 3:
                        half = (k - K_MEMV) // 4
                        if half:
                            act.wait_ge(sem["mv_out0"], 16)
                        for m in range(2):
                            act.activation(vst[:, m, :], bank[2 * half + m][:], ACT.Copy).then_inc(sem["mv_ready"], 1)

                fill(K_MEMK)
                act.wait_ge(sem["btok_done"], 1)
                act.activation(btok[:].rearrange("p c n -> p (c n)"), bank[5][:], ACT.Copy).then_inc(sem["btok_ready"], 1)
                for c in range(2):
                    act.wait_ge(sem["xtok_done"], c + 1)
                    act.activation(xtok[:, c, :], bank[6 + c][:], ACT.Copy).then_inc(sem["xtok_ready"], 1)
                fill(K_MEMK + 1)

                def decays(h):
                    act.wait_ge(sem["d_ready"], h + 1)
                    act.activation(dec[:, h, :], dbuf[:, h % 2, 384:392], ACT.Exp)
                    act.activation(dbuf[:, h % 2, 0:384], dbuf[:, h % 2, 0:384], ACT.Exp).then_inc(sem["e_ready"], 1)

                decays(0)
                decays(1)
                fill(K_MEMK + 2)
                for i in range(3):
                    decays(2 * i + 2)
                    decays(2 * i + 3)
                    fill(K_MEMK + 3 + i)
                act.wait_ge(sem["ssdp_done"], 1)
                act.activation(ssdo[:], bank[6][:], ACT.Copy).then_inc(sem["ssdp_ready"], 1)
                fill(K_MEMK + 6)
                fill(K_MEMK + 7)
                fill(K_MEMV)
                fill(K_MEMV + 1)
                act.wait_ge(sem["ssd_gated"], 4)
                act.activation(sq4[:], yg[:, 0:4, :], ACT.Square).then_inc(sem["ssd_sq"], 1)
                for g in range(2):
                    act.wait_ge(sem["sg_done"], g + 1)
                    link(act.activation(rn[:, g, :], bank[6 + g][:, 0:T], ACT.Ln, scale=1.0 / 256, bias=cc("eps")))
                    act.activation(rn[:, g, :], rn[:, g, :], ACT.Exp, scale=-0.5).then_inc(sem["sg_r"], 1)
                act.wait_ge(sem["vt_done"], 1)
                act.activation(gvtok[:].rearrange("p c n -> p (c n)"), bank[5][:], ACT.Copy).then_inc(sem["vt_ready"], 1)
                act.wait_ge(sem["ssdp_out"], 16)
                act.wait_ge(sem["vt_done"], 2)
                act.activation(rvtok[:].rearrange("p c n -> p (c n)"), bank[4][:], ACT.Copy).then_inc(sem["vt_ready"], 1)
                fill(K_MEMV + 2)
                act.wait_ge(sem["d9_ready"], 1)
                link(act.activation(ke[:], ke[:], ACT.Abs))
                act.activation(ke[:], ke[:], ACT.Exp, scale=-1.0).then_inc(sem["e9_ready"], 1)
                act.activation(gdec[:], glog[:, TP:T], ACT.Exp).then_inc(sem["gdec_ready"], 1)
                act.wait_ge(sem["rkt_done"], 1)
                act.activation(rktok[:].rearrange("p a c n -> p (a c n)"), bank[4][:], ACT.Copy).then_inc(sem["rktok_ready"], 1)
                act.wait_ge(sem["gkt_done"], 1)
                act.activation(gktok[:].rearrange("p c n -> p (c n)"), bank[7][:, 0:TP], ACT.Copy).then_inc(sem["gkt_ready"], 1)
                for k in range(K_MEMV + 3, K_WOUT):
                    fill(k)

                act.wait_ge(sem["gy_evac"], 4)
                act.activation(sq4[:, 0:2, :], yb[:, 0:2, :], ACT.Square).then_inc(sem["gsq_ready"], 1)
                for i in range(2):
                    act.wait_ge(sem["gms_done"], i + 1)
                    link(act.activation(rn[:, i, :], bank[4 + i][:, 0:T], ACT.Ln, bias=cc("eps")))
                    act.activation(rn[:, i, :], rn[:, i, :], ACT.Exp, scale=-0.5).then_inc(sem["gms_r"], 1)
                act.wait_ge(sem["ry_evac"], 6)
                act.activation(sq4[:, 2:4, :], yb[:, 2:4, :], ACT.Square).then_inc(sem["gsq_ready"], 1)
                for i in range(2):
                    act.wait_ge(sem["gms_done"], i + 3)
                    link(act.activation(rn[:, 2 + i, :], bank[4 + i][:, 0:T], ACT.Ln, bias=cc("eps")))
                    act.activation(rn[:, 2 + i, :], rn[:, 2 + i, :], ACT.Exp, scale=-0.5).then_inc(sem["gms_r"], 1)

                act.wait_ge(sem["ssds_out"], 16)
                for b in range(KB):
                    if b in (0, 4, 6):
                        act.wait_ge(sem["y_final"], {0: 4, 4: 6, 6: 8}[b])
                    act.activation(xn_hi[:, b, :], yg[:, b, :], ACT.Copy).then_inc(sem["y_hi"], 1)
                for m in range(KB):
                    ahead(K_WOUT + m)

                norm_parts(2)
                norm_scale(2)
                for m in range(KB):
                    ahead(K_Q + m)

                def softmax(h):
                    act.wait_ge(sem["mx_ready"], h + 1)
                    if h >= 2:
                        act.wait_ge(sem["pt_done"], h - 1)
                    for c in range(2):
                        act.activation(pr[:, h % 2, c, :], bank[h % 2][:, c * TP:c * TP + TP], ACT.Exp, bias=nmx[:, h, c:c + 1],
                                       scale=1.0 / 16, accum_out=psm[:, h, c:c + 1]).then_inc(sem["p_ready"], 1)

                def probs_out(h):
                    act.wait_ge(sem["pt_done"], h + 1)
                    act.activation(prt[:, h % 2, :, :].rearrange("p m l -> p (m l)"), bank[2 + h % 2][:], ACT.Copy).then_inc(sem["prt_ready"], 1)

                def attended(h):
                    act.wait_ge(sem["pv_done"], h + 1)
                    for i in range(2):
                        act.activation(xn_hi[:, 2 * h + i, 0:TP], bank[4 + h % 2][:, i * TP:i * TP + TP], ACT.Copy).then_inc(sem["o_hi"], 1)

                softmax(0)
                for h in range(HEADS):
                    if h < HEADS - 1:
                        softmax(h + 1)
                    probs_out(h)
                    attended(h)
                act.wait_ge(sem["ss_mx"], 1)
                act.activation(ps_s[:], bank[6][0:32, 0:TP], ACT.Exp, bias=m32[:, 1:2], scale=1.0 / 16,
                               accum_out=m32[:, 2:3]).then_inc(sem["ss_p"], 1)
                act.wait_ge(sem["kv_used"], 2 * NS)
                act.activation(os_s[:], bank[6][0:32, 0:TP], ACT.Copy).then_inc(sem["ss_o"], 1)
                act.wait_ge(sem["ss_t3"], 1)
                for i in range(2):
                    act.activation(xn_hi[:, i:KB:2, TP:T], bank[7][:, 64 + 32 * i:96 + 32 * i].rearrange("p (b h) -> p h b", h=HEADS),
                                   ACT.Copy).then_inc(sem["o_hi"], 1)
                for m in range(KB):
                    ahead(K_O + m)

                ffn(1)
                layer_end(act, "act")

            chain[0] = 0
            for b in range(KB):
                act.activation(sq[:, b, :], x[:, b, :], ACT.Square).then_inc(sem["sq_ready"], 1)
            norm_scale(0)

        @block.vector
        def _(dve):
            chain = [0]

            def link(ins):
                chain[0] += 1
                ins.then_inc(sem["dve_chain"], 1)
                dve.wait_ge(sem["dve_chain"], chain[0])

            def over(ap, count):
                return ap.unsqueeze(2).to_broadcast([ap.shape[0], ap.shape[1], count])

            def each(ap, count):
                return ap.unsqueeze(1).to_broadcast([ap.shape[0], count, ap.shape[1]])

            def norm_low(n):
                for b in range(KB):
                    dve.wait_ge(sem["xn_hi"], KB * n + b + 1)
                    dve.scalar_tensor_tensor(xn_lo[:, b, :], x[:, b, :], pc(f"n{n + 1}", b, b + 1), xn_hi[:, b, :].bitcast(F32),
                                             ALU.mult, ALU.subtract).then_inc(sem["xn_lo"], 1)

            def ffn(f):
                k0 = (K_FFN1, K_FFN2)[f]
                norm_low((0, 3)[f])
                dve.wait_ge(sem["r_ready"], (1, 4)[f])
                with dve.Fori(0, 2) as half:
                    k = half * HALF_CH + k0
                    b = half * HALF + 2 * HALF * f

                    def low(j):
                        dve.wait_ge(sem["hhi_ready"], b + (j + 1))
                        dve.tensor_tensor(h_lo[:, j, :], h32[:, j % 2, :], h_hi[:, j, :].bitcast(F32), ALU.subtract).then_inc(sem["h_ready"], 1)

                    for j in range(HALF):
                        dve.wait_ge(sem["chunk_used"], k + (2 * j + 2))
                        dve.tensor_tensor(gbuf[:, j % 2, :], bank[2 * (j % 2)][:, 0:T], r_bc[:], ALU.mult).then_inc(sem["g_ready"], 1)
                        dve.tensor_tensor(ubuf[:, j % 2, :], bank[2 * (j % 2) + 1][:, 0:T], r_bc[:], ALU.mult).then_inc(sem["up_evac"], 1)
                        if j:
                            low(j - 1)
                        dve.wait_ge(sem["s_ready"], b + (j + 1))
                        dve.wait_ge(sem["up_evac"], b + (j + 1))
                        dve.tensor_tensor(h32[:, j % 2, :], sbuf_[:, j % 2, :], ubuf[:, j % 2, :], ALU.mult).then_inc(sem["h32_ready"], 1)
                    low(HALF - 1)
                    for m in range(KB):
                        if m < KB - 1:
                            dve.wait_ge(sem["down_done"], half * (KB - 1) + (2 * (KB - 1) * f + m + 1))
                        else:
                            dve.wait_ge(sem["chunk_used"], k + HALF_CH)
                        dve.scalar_tensor_tensor(x[:, m, :], bank[4 + m % 4][:, 0:T], 0.5, x[:, m, :], ALU.mult, ALU.add).then_inc(sem["x_done"], 1)

            dve.wait_ge(loaded, 64)
            dve.wait_ge(mem_split, 1)
            dve.tensor_tensor(mem_lo[:], mem_raw[:], mem_hi[:].bitcast(F32), ALU.subtract).then_inc(mem_split, 1)
            with dve.Fori(0, depth):
                chain[0] = 0
                ffn(0)

                dve.memset(xp[:, :, 0:3], 0.0).then_inc(sem["conv_out_ready"], 1)
                dve.wait_ge(sem["st_in"], 48)
                seg = xp[:, :, TP + 3:PADW].rearrange("p k (b j) -> p k b j", j=4)
                link(dve.tensor_copy(seg[:, :, :, 0:3], convld[:]))
                norm_low(1)
                dve.wait_ge(sem["ws_hi_ready"], 1)
                dve.tensor_tensor(ws_lo[:], pc("ws"), ws_hi[:].bitcast(F32), ALU.subtract).then_inc(sem["ws_ready"], 1)
                dve.wait_ge(sem["r_ready"], 2)

                def evac(n, *pairs, scale=None):
                    dve.wait_ge(sem["chunk_used"], K_WIN + n + 1)
                    for i, (dst, cols) in enumerate(pairs):
                        src = bank[n % 4][:, cols[0]:cols[1]]
                        if scale is None:
                            ins = dve.tensor_tensor(dst, src, r_bc[:, cols[0]:cols[1]], ALU.mult)
                        else:
                            ins = dve.scalar_tensor_tensor(dst, src, scale, r_bc[:, cols[0]:cols[1]], ALU.mult, ALU.mult)
                    ins.then_inc(sem["win_evac"], 1)

                for n in range(8):
                    evac(n, (xp[:, n, 3:TP + 3], (0, TP)), (seg[:, n, :, 3], (TP, T)))
                    dve.wait_ge(sem["win_evac"], n + 1)
                    if n >= 2:
                        dve.wait_ge(sem["xs_ready"], n - 1)
                    w = lambda j: pc("cw", 4 * n + j, 4 * n + j + 1)
                    link(dve.tensor_scalar(cbuf[:, n % 2, :], xp[:, n, 0:288], w(0), pc("cb", n, n + 1), ALU.mult, ALU.add))
                    for j in range(1, 4):
                        ins = dve.scalar_tensor_tensor(cbuf[:, n % 2, :], xp[:, n, j:j + 288], w(j), cbuf[:, n % 2, :], ALU.mult, ALU.add)
                        if j < 3:
                            link(ins)
                    ins.then_inc(sem["conv_done"], 1)
                    if n == 0:
                        dve.wait_ge(sem["small_done"], 1)
                        dve.tensor_tensor(sm[:], bank[7][0:SM, 0:T], r_bc[0:SM, :], ALU.mult).then_inc(sem["small_evac"], 1)
                dve.tensor_copy(convst[:, :, 0, :], xp[:, :, TP:TP + 3])
                dve.tensor_copy(convst[:, :, 1:9, :], seg[:, :, :, 1:4]).then_inc(sem["conv_out_ready"], 1)
                for n in range(8, 12):
                    evac(n, (yg[:, n - 8, :], (0, T)))
                v8 = sm[0:8, :]
                dve.wait_ge(sem["small_evac"], 1)
                link(dve.tensor_scalar(v8, v8, pc("dtb", rows=slice(0, 8)), None, ALU.add))
                dve.scalar_tensor_tensor(sp[0][0:8, :], v8, -1.0, v8, ALU.mult, ALU.min).then_inc(sem["lp_dve"], 1)
                dve.wait_ge(sem["gate_done"], 1)
                link(dve.tensor_scalar(vg[:], bank[6][:, 0:T], pc("glab"), None, ALU.add))
                dve.scalar_tensor_tensor(ng[:], vg[:], -1.0, vg[:], ALU.mult, ALU.min).then_inc(sem["lp_dve"], 1)
                evac(12, (qkv[:, 0, :], (0, T)), scale=32.0 ** -0.5)
                evac(13, (qkv[:, 1, :], (0, T)))
                evac(14, (qkv[:, 2, :], (0, T)))
                for s, (e, u, w) in enumerate(((e8[:], dt8[:], sp[0][0:8, :]), (eg, ug, ng[:]))):
                    dve.wait_ge(sem["lp_act"], 1 + s)
                    link(dve.tensor_scalar(u, e, 1.0, None, ALU.add))
                    dve.scalar_tensor_tensor(w, u, 1.0, e, ALU.subtract, ALU.subtract).then_inc(sem["lp_dve"], 1)
                evac(15, (qkv[:, 3, :], (0, T)))
                evac(16, (qkv[:, 4, :], (0, T)))
                dve.wait_ge(sem["lp_act"], 3)
                dve.wait_ge(sem["lp_dve"], 4)
                link(dve.tensor_tensor(e8[:], e8[:], sp[0][0:8, :], ALU.subtract))
                link(dve.scalar_tensor_tensor(dt8[:], v8, 0.0, e8[:], ALU.max, ALU.add))
                dve.wait_ge(sem["z_ready"], 1)
                link(dve.tensor_scalar(la8[:], dt8[:], na8[:], -1.0, ALU.mult, ALU.mult))
                dve.tensor_copy(bsum[:, TP:T], la8[:, TP:T])
                dve.tensor_tensor_scan(bsum[:, 0:TP], cc("ones", 0, 1, rows=slice(0, 8)).to_broadcast([8, TP]), la8[:, 0:TP], 0.0,
                                       ALU.mult, ALU.add).then_inc(sem["bsum_ready"], 1)
                dve.wait_ge(sem["lp_act"], 4)
                link(dve.tensor_tensor(eg, eg, ng[:], ALU.subtract))
                link(dve.scalar_tensor_tensor(eg, vg[:], 0.0, eg, ALU.min, ALU.subtract))
                link(dve.tensor_scalar(eg, eg, 1.0 / 16, None, ALU.mult))
                dve.tensor_copy(glog[:, TP:T], eg[:, TP:T])
                link(dve.tensor_tensor_scan(glog[:, 0:TP], cc("ones", 0, 1).to_broadcast([P, TP]), eg[:, 0:TP], 0.0, ALU.mult, ALU.add))
                for n in range(17, 20):
                    evac(n, (qkv[:, n - 12, :], (0, T)))
                    if n in (17, 19):
                        a = n - 13
                        dve.wait_ge(sem["win_evac"], n + 1)
                        ab = qkv[:, a:a + 2, :]
                        dve.tensor_tensor(rp[0][:], ab, each(cc("cos"), 2), ALU.mult)
                        link(dve.tensor_tensor(rp[1][:], ab, each(cc("sin"), 2), ALU.mult))
                        dve.tensor_tensor(qkv[:, a, :], rp[0][:, 0, :], rp[1][:, 1, :], ALU.subtract)
                        link(dve.tensor_tensor(qkv[:, a + 1, :], rp[0][:, 1, :], rp[1][:, 0, :], ALU.add))
                for n in range(20, 22):
                    evac(n, (qkv[:, n - 12, :], (0, T)))
                for n in range(22, N_WIN):
                    evac(n, (yg[:, n - 18, :], (0, T)))

                dve.wait_ge(sem["bs_done"], 1)
                dve.tensor_copy(bs[:].rearrange("p c h -> p (c h)"), bank[4][:, 0:16]).then_inc(sem["bs_ready"], 1)
                dve.wait_ge(sem["xs_ready"], 8)
                for i in range(4):
                    dve.wait_ge(sem["dtb_done"], i + 1)
                    dve.tensor_tensor(xdt[:, i, :], xc[:, i, :], bank[(5, 6, 7, 4)[i]][:, 0:T], ALU.mult).then_inc(sem["xdt_ready"], 1)
                for g in range(2):
                    dve.wait_ge(sem["g_done"], g + 1)
                    dve.tensor_tensor(gm[:, g, :], bank[4 + g][:, 0:384], cc("tri"), ALU.mult).then_inc(sem["gm_ready"], 1)

                def diffs(h):
                    dve.wait_ge(sem["bc_done"], h + 1)
                    dve.wait_ge(sem["bs_ready"], 1)
                    if h >= 2:
                        dve.wait_ge(sem["m_ready"], h - 1)
                    src, d = bank[6 + h % 2], dbuf[:, h % 2, :]
                    dve.tensor_scalar(d[:, 0:TP], src[:, 0:TP], bs[:, 0, h:h + 1], 0.0, ALU.subtract, ALU.min)
                    dve.tensor_scalar(d[:, TP:384], src[:, P:TP], bs[:, 1, h:h + 1], 0.0, ALU.subtract, ALU.min)
                    dve.tensor_copy(d[:, 384:392], src[:, TP:T]).then_inc(sem["d_ready"], 1)

                def decayed(h):
                    dve.wait_ge(sem["e_ready"], h + 1)
                    dve.wait_ge(sem["gm_ready"], 2)
                    if h >= 2:
                        dve.wait_ge(sem["y_done"], h - 1)
                    d, hc = dbuf[:, h % 2, :], slice(64 * h, 64 * h + 64)
                    dve.wait_ge(sem["xtok_ready"], 2)
                    for c in range(2):
                        dve.tensor_scalar(xtail[:, c, hc], xtok[:, c, hc], d[:, 255 + P * c:256 + P * c], None, ALU.mult)
                    dve.tensor_tensor(mbuf[:, h % 2, :], d[:, 0:384], gm[:, h // 4, :], ALU.mult).then_inc(sem["m_ready"], 1)

                def skip(i):
                    dve.wait_ge(sem["y_done"], 2 * i + 2)
                    dve.scalar_tensor_tensor(xc[:, i, 0:TP], xc[:, i, 0:TP], pc("dsk", i, i + 1), bank[4 + i % 2][:, 0:TP],
                                             ALU.mult, ALU.add).then_inc(sem["y_evac"], 1)

                diffs(0)
                diffs(1)
                for h in range(HEADS_S):
                    decayed(h)
                    if h + 2 < HEADS_S:
                        diffs(h + 2)
                    if h % 2 and h > 1:
                        skip(h // 2 - 1)
                skip(3)
                dve.wait_ge(sem["st_ssd_in"], 16)
                for i in range(4):
                    b_col, s_i = xc[:, 4 + i // 2, TP:T], sst[:, i, :, :]
                    if i:
                        dve.wait_ge(sem["xb_done"], i)
                    dve.wait_ge(sem["xdt_ready"], 4)
                    dve.tensor_tensor(xe[:], over(xdt[:, i, TP:T], P), each(ident, NS), ALU.mult).then_inc(sem["xe_ready"], 1)
                    for q in range(2):
                        dve.tensor_tensor(s_i[:, :, 64 * q:64 * q + 64], s_i[:, :, 64 * q:64 * q + 64], over(dec[:, 2 * i + q, :], 64), ALU.mult)
                    dve.wait_ge(sem["xb_done"], i + 1)
                    for q in range(2):
                        ins = dve.tensor_tensor(tb[:, 4 * q:4 * q + 4, :], bank[6 + q][:].rearrange("p (b n) -> p b n", n=P),
                                                over(b_col[:, 4 * q:4 * q + 4], P), ALU.mult)
                    ins.then_inc(sem["xb_evac"], 1)
                    dve.wait_ge(sem["xb_evac"], i + 1)
                    dve.tensor_tensor(s_i, s_i, tb[:], ALU.add).then_inc(sem["sst_ready"], 1)
                dve.wait_ge(sem["z_ready"], 2)
                dve.wait_ge(sem["y_evac"], 4)
                dve.wait_ge(sem["o_done"], 1)
                for i in range(4):
                    link(dve.scalar_tensor_tensor(xc[:, i, TP:T], xc[:, i, TP:T], pc("dsk", i, i + 1), bank[4][:, NS * i:NS * i + NS], ALU.mult, ALU.add))
                    dve.tensor_tensor(yg[:, i, :], yg[:, i, :], xc[:, i, :], ALU.mult).then_inc(sem["ssd_gated"], 1)

                dve.wait_ge(sem["ssdp_done"], 1)
                dve.wait_ge(sem["sg_r"], 2)
                for i in range(4):
                    dve.wait_ge(sem["sg_r"], i // 2 + 1)
                    dve.scalar_tensor_tensor(yg[:, i, :], yg[:, i, :], pc("ssdw", i, i + 1), rn[:, i // 2, :], ALU.mult, ALU.mult).then_inc(sem["y_final"], 1)
                dve.wait_ge(sem["y_final"], 4)
                for l, span in enumerate(LEVELS):
                    pairs = glog[:, 0:TP].rearrange("p (n s) -> p n s", s=2 * span)
                    ref = pairs[:, :, span - 1:span].to_broadcast([P, TP // (2 * span), 2 * span])
                    dve.tensor_tensor(ke[:, l, :].rearrange("p (n s) -> p n s", s=2 * span), pairs, ref, ALU.subtract)
                dve.tensor_scalar(ke[:, 8, :], glog[:, 0:TP], glog[:, TP - 1:TP], None, ALU.subtract).then_inc(sem["d9_ready"], 1)
                dve.wait_ge(sem["vt_ready"], 1)
                rkt = gtmp[:].rearrange("p (a t) -> p a t", a=2)
                dve.tensor_tensor(rkt, qkv[:, 6:8, 0:TP], each(cc("rtail"), 2), ALU.mult).then_inc(sem["rkt_ready"], 1)
                dve.wait_ge(sem["e9_ready"], 1)
                link(dve.tensor_tensor(qe[:], ke[:, 0:8, :], each(qkv[:, 0, 0:TP], 8), ALU.mult))
                dve.tensor_tensor(ke[:], ke[:], each(qkv[:, 1, 0:TP], 9), ALU.mult).then_inc(sem["ke_ready"], 1)
                dve.wait_ge(sem["rktok_ready"], 1)

                evacs = [0]
                for h in range(HEADS):
                    m3 = mg[:, h % 2, :]
                    acc = m3.rearrange("p (c n) -> p c n", n=P)[:, 0:3:2, :]
                    if h >= 2:
                        dve.wait_ge(sem["gy_done"], h - 1)
                    for r in range(4):
                        dve.wait_ge(sem["lv_done"], 5 * h + r + 1)
                        for l in range(2):
                            mask = each(cc("lmask", P * (2 * r + l), P * (2 * r + l) + P), 2)
                            src = bank[4 + (5 * h + r) % 2][:, 256 * l:256 * l + 256].rearrange("p (c n) -> p c n", n=P)
                            if r == 0 and l == 0:
                                link(dve.tensor_tensor(acc, src, mask, ALU.mult))
                            else:
                                ins = dve.tensor_tensor(gtmp[:, 0:256].rearrange("p (c n) -> p c n", n=P), src, mask, ALU.mult)
                                if l:
                                    evacs[0] += 1
                                    ins.then_inc(sem["lv_evac"], 1)
                                    dve.wait_ge(sem["lv_evac"], evacs[0])
                                else:
                                    link(ins)
                                link(dve.tensor_tensor(acc, acc, gtmp[:, 0:256].rearrange("p (c n) -> p c n", n=P), ALU.add))
                    dve.wait_ge(sem["lv_done"], 5 * h + 5)
                    evacs[0] += 1
                    dve.tensor_copy(m3[:, P:TP], bank[4 + (5 * h + 4) % 2][:, 0:P]).then_inc(sem["lv_evac"], 1)
                    dve.wait_ge(sem["lv_evac"], evacs[0])
                    dve.sem_inc(sem["mg_ready"], 1)
                dve.wait_ge(sem["gy_done"], 4)
                dve.tensor_copy(yb[:, 0:2, 0:TP], bank[6][:].rearrange("p (i t) -> p i t", i=2)).then_inc(sem["gy_evac"], 1)
                dve.wait_ge(sem["gs_done"], 1)
                for h in range(HEADS):
                    rows = slice(32 * h, 32 * h + 32)
                    dve.tensor_copy(sto[rows, 0, :], bank[7][rows, 64 * h:64 * h + 64]).then_inc(sem["gs_ready"], 1)

                for h in range(HEADS):
                    dve.wait_ge(sem["rsc_done"], h + 1)
                    if h < 2:
                        dve.wait_ge(sem["gy_done"], 4)
                    else:
                        dve.wait_ge(sem["ry_done"], h - 1)
                    dve.tensor_tensor(mg[:, h % 2, :], bank[4 + h % 2][:, 0:384], cc("decay", 384 * h, 384 * h + 384), ALU.mult).then_inc(sem["mr_ready"], 1)
                dve.wait_ge(sem["ry_done"], 4)
                dve.tensor_copy(yb[:, 2:4, 0:TP], bank[7][:].rearrange("p (i t) -> p i t", i=2)).then_inc(sem["ry_evac"], 1)
                dve.wait_ge(sem["rs_done"], 1)
                for j in range(2):
                    for h in range(HEADS):
                        rows = slice(32 * h, 32 * h + 32)
                        dve.tensor_copy(sto[rows, 1 + j, :], bank[6][rows, TP * j + 64 * h:TP * j + 64 * h + 64]).then_inc(sem["gs_ready"], 1)

                for kind in range(2):
                    v0 = (2, 8)[kind]
                    if kind:
                        dve.wait_ge(sem["vb_done"], 1)
                    for i in range(2):
                        dve.tensor_tensor(xg[:, i, :, :], over(qkv[:, v0 + i, TP:T], 64), each(cc("id64"), NS), ALU.mult).then_inc(sem["xg_ready"], 1)
                    for j in range(1 + kind):
                        s_j = gst[:] if kind == 0 else rst[:, j, :, :]
                        q_col, k_col = (qkv[:, 0, TP:T], qkv[:, 1, TP:T]) if kind == 0 else (qkv[:, 4 + j, TP:T], qkv[:, 6 + j, TP:T])
                        dve.tensor_tensor(qx[:, kind + j, :, :], over(q_col, 4), each(cc("hmask"), NS), ALU.mult).then_inc(sem["qx_ready"], 1)
                        if kind == 0:
                            dve.wait_ge(sem["gdec_ready"], 1)
                            link(dve.tensor_tensor(s_j, s_j, over(gdec[:], 64), ALU.mult))
                        else:
                            link(dve.tensor_scalar(s_j, s_j, cc("gamma"), None, ALU.mult))
                        dve.wait_ge(sem["vb_done"], kind + 1)
                        link(dve.tensor_tensor(tg[:], bank[4 + 2 * kind][:].rearrange("p (b n) -> p b n", n=64), over(k_col, 64), ALU.mult))
                        link(dve.scalar_tensor_tensor(s_j, tg[:], (1.0, 0.125)[kind], s_j, ALU.mult, ALU.add))
                        dve.sem_inc(sem["gst_ready"], 1)
                for kind in range(2):
                    dve.wait_ge(sem["go_done"], kind + 1)
                    for i in range(2):
                        dve.tensor_copy(yb[:, 2 * kind + i, TP:T], bank[5 if kind == 0 else 7][:, NS * i:NS * i + NS])\
                           .then_inc(sem[("gy_evac", "ry_evac")[kind]], 1)
                    if kind == 0:
                        dve.wait_ge(sem["gy_evac"], 3)
                        dve.sem_inc(sem["gy_evac"], 1)
                for i in range(2):
                    dve.wait_ge(sem["mu_done"], i + 1)
                    if i == 0:
                        dve.wait_ge(sem["ry_evac"], 3)
                    dve.tensor_tensor(yb[:, 2 + i, :], yb[:, 2 + i, :], bank[6 + i][:, 0:T], ALU.subtract).then_inc(sem["ry_evac"], 1)
                dve.wait_ge(sem["ry_evac"], 5)
                dve.sem_inc(sem["ry_evac"], 1)
                dve.wait_ge(sem["gg_ready"], 1)
                for kind in range(2):
                    for i in range(2):
                        dve.wait_ge(sem["gms_r"], 2 * kind + i + 1)
                        y_i = yb[:, 2 * kind + i, :]
                        link(dve.scalar_tensor_tensor(y_i, y_i, pc(("glaw", "retw")[kind], i, i + 1), rn[:, 2 * kind + i, :], ALU.mult, ALU.mult))
                        dve.tensor_tensor(yg[:, 4 + 2 * kind + i, :], yg[:, 4 + 2 * kind + i, :], y_i, ALU.mult)\
                           .then_inc(sem["y_final"], 1)

                for b in range(KB):
                    dve.wait_ge(sem["y_hi"], b + 1)
                    dve.tensor_tensor(xn_lo[:, b, :], yg[:, b, :], xn_hi[:, b, :].bitcast(F32), ALU.subtract).then_inc(sem["y_lo"], 1)

                def residual(k, m):
                    dve.wait_ge(sem["chunk_used"], k + m + 1)
                    dve.tensor_tensor(x[:, m, :], x[:, m, :], bank[m % 4][:, 0:T], ALU.add).then_inc(sem["x_done"], 1)

                for m in range(KB):
                    residual(K_WOUT, m)
                    if m == 3:
                        dve.wait_ge(sem["mix_out"], 64)
                        for i in range(2):
                            dve.memset(apart[i][:], 0.0).then_inc(sem["ss_zero"], 1)

                norm_low(2)
                dve.wait_ge(sem["r_ready"], 3)
                for m in range(KB):
                    dve.wait_ge(sem["chunk_used"], K_Q + m + 1)
                    dve.tensor_tensor(qt[:, m, :], bank[m % 4][:, 0:T], r_bc[:], ALU.mult).then_inc(sem["q_ready"], 1)

                dve.wait_ge(sem["q_ready"], KB)
                dve.wait_ge(sem["ss_zero"], 2)
                for i in range(2):
                    dve.tensor_copy(apart[i][:, 31:1024:32].rearrange("p (k b) -> p k b", b=NS), qt[:, 4 * i:4 * i + 4, TP:T]).then_inc(sem["ss_q"], 1)

                def head_max(h):
                    dve.wait_ge(sem["sc_done"], h + 1)
                    link(dve.tensor_reduce(mx[:, h, :], bank[h % 2][:].rearrange("p (c m) -> p c m", c=2), AX.X, ALU.max))
                    dve.tensor_scalar(nmx[:, h, :], mx[:, h, :], -1.0 / 16, None, ALU.mult).then_inc(sem["mx_ready"], 1)

                def head_norm(h):
                    dve.wait_ge(sem["p_ready"], 2 * h + 2)
                    link(dve.reciprocal(rsm[:, h, :], psm[:, h, :]))
                    for c in range(2):
                        dve.tensor_scalar(pr[:, h % 2, c, :], pr[:, h % 2, c, :], rsm[:, h, c:c + 1], None, ALU.mult).then_inc(sem["pn_ready"], 1)

                def head_low(h):
                    dve.wait_ge(sem["o_hi"], 2 * h + 2)
                    for i in range(2):
                        dve.tensor_tensor(xn_lo[:, 2 * h + i, 0:TP], bank[4 + h % 2][:, i * TP:i * TP + TP],
                                          xn_hi[:, 2 * h + i, 0:TP].bitcast(F32), ALU.subtract).then_inc(sem["o_lo"], 1)

                head_max(0)
                for h in range(HEADS):
                    head_norm(h)
                    if h < HEADS - 1:
                        head_max(h + 1)
                    head_low(h)
                dve.wait_ge(sem["kv_used"], NS)
                link(dve.tensor_reduce(m32[:, 0:1], bank[6][0:32, 0:TP], AX.X, ALU.max))
                dve.tensor_scalar(m32[:, 1:2], m32[:, 0:1], -1.0 / 16, None, ALU.mult).then_inc(sem["ss_mx"], 1)
                dve.wait_ge(sem["ss_p"], 1)
                link(dve.reciprocal(m32[:, 3:4], m32[:, 2:3]))
                dve.tensor_scalar(ps_s[:], ps_s[:], m32[:, 3:4], None, ALU.mult).then_inc(sem["ss_pn"], 1)
                dve.wait_ge(sem["ss_t2"], 1)
                dve.tensor_copy(apart[0][:, 31:1024:32], bank[7][:, 0:32])
                dve.tensor_copy(apart[1][:, 31:1024:32], bank[7][:, 32:64]).then_inc(sem["ss_pts"], 1)
                dve.wait_ge(sem["o_hi"], KB + 2)
                for i in range(2):
                    dve.tensor_tensor(xn_lo[:, i:KB:2, TP:T], bank[7][:, 64 + 32 * i:96 + 32 * i].rearrange("p (b h) -> p h b", h=HEADS),
                                      xn_hi[:, i:KB:2, TP:T].bitcast(F32), ALU.subtract).then_inc(sem["o_lo"], 1)
                for m in range(KB):
                    residual(K_O, m)

                ffn(1)
                layer_end(dve, "dve")

            dve.wait_ge(sem["r_ready"], 1)
            for b in range(KB):
                dve.scalar_tensor_tensor(yo[:, b, :], x[:, b, :], pc("n1", b, b + 1), r_bc[:], ALU.mult, ALU.mult).then_inc(sem["h_ready"], 1)

        @block.tensor
        def _(pe):
            def mm3(out, w, tile, moving, cols, start, stop, wide=False):
                a, b = tile
                hi, lo = moving
                pe.matmul(out, w[0][:, a:b], hi[:, cols[0]:cols[1]], start=start, stop=False)
                pe.matmul(out, w[0][:, a:b], lo[:, cols[0]:cols[1]], start=False, stop=False)
                return pe.matmul(out, w[1][:, a:b], hi[:, cols[0]:cols[1]], start=False, stop=stop)

            def parts(k):
                return w_hi[:, k % SPL, :], w_lo[:, k % SPL, :]

            def project(k, out, hi, lo, n=T):
                pe.wait_ge(lo_ready, k + 1)
                for b in range(KB):
                    ins = mm3(out[:, 0:n], parts(k), (P * b, P * b + P), (hi[:, b, :], lo[:, b, :]), (0, n), b == 0, b == KB - 1)
                ins.then_inc(sem["chunk_used"], 1)

            def token_sums(n):
                if n:
                    pe.wait_ge(sem["r_ready"], n)
                for b in range(KB):
                    pe.wait_ge(sem["sq_ready"], KB * n + b + 1)
                    ins = pe.matmul(SUMS[n][:, 0:T], ones, sq[:, b, :], start=b == 0, stop=b == KB - 1)
                ins.then_inc(sem["ss_ready"], 1)

            def ffn(f):
                k0 = (K_FFN1, K_FFN2)[f]
                token_sums((0, 3)[f])
                pe.wait_ge(sem["xn_lo"], (KB, 4 * KB)[f])
                if f:
                    pe.wait_ge(sem["x_done"], X_DONE[3])
                with pe.Fori(0, 2) as half:
                    k = half * HALF_CH + k0
                    b = half * HALF + 2 * HALF * f
                    for j in range(HALF):
                        if j >= 2:
                            pe.wait_ge(sem["up_evac"], b + (j - 1))
                        for u in range(2):
                            pe.wait_ge(lo_ready, k + (2 * j + u + 1))
                            for i in range(KB):
                                ins = mm3(bank[2 * (j % 2) + u][:, 0:T], parts(2 * j + u), (P * i, P * i + P),
                                          (xn_hi[:, i, :], xn_lo[:, i, :]), (0, T), i == 0, i == KB - 1)
                            ins.then_inc(sem["chunk_used"], 1)
                    for t in range(KB * HALF):
                        c, (m, i) = 2 * HALF + t // TILES, divmod(t, HALF)
                        if t % TILES == 0:
                            pe.wait_ge(lo_ready, k + (c + 1))
                        if m == 0:
                            pe.wait_ge(sem["h_ready"], b + (i + 1))
                        if m >= 4 and i == 0:
                            pe.wait_ge(sem["x_done"], half * KB + (32 * f + m - 3))
                        a = P * (t % TILES)
                        ins = mm3(bank[4 + m % 4][:, 0:T], parts(c), (a, a + P), (h_hi[:, i, :], h_lo[:, i, :]), (0, T), i == 0, i == HALF - 1)
                        if t % TILES == TILES - 1:
                            ins.then_inc(sem["chunk_used"], 1)
                        elif i == HALF - 1:
                            ins.then_inc(sem["down_done"], 1)

            pe.wait_ge(loaded, 64)
            with pe.Fori(0, depth):
                ffn(0)

                token_sums(1)
                pe.wait_ge(sem["xn_lo"], 2 * KB)
                pe.wait_ge(sem["x_done"], 16)
                for n in range(N_WIN):
                    if n == 3:
                        pe.wait_ge(sem["r_ready"], 2)
                    if n >= 4:
                        pe.wait_ge(sem["win_evac"], n - 3)
                    project(K_WIN + n, bank[n % 4], xn_hi, xn_lo)
                    if n == 0:
                        pe.wait_ge(sem["ws_ready"], 1)
                        for b in range(KB):
                            ins = mm3(bank[7][:, 0:T], (ws_hi, ws_lo), (SM * b, SM * b + P), (xn_hi[:, b, :], xn_lo[:, b, :]), (0, T), b == 0, b == KB - 1)
                        ins.then_inc(sem["small_done"], 1)
                    if n == 2:
                        pe.wait_ge(sem["small_evac"], 1)
                        pe.wait_ge(sem["r_ready"], 2)
                        pe.matmul(bank[6][:, 0:T], pc("gwg", rows=slice(32, 48)), sm[32:48, :], start=True, stop=True).then_inc(sem["gate_done"], 1)

                def fill(k):
                    if k < K_MEMV:
                        m = k - K_MEMK
                        if m < 4:
                            pe.wait_ge(sem["win_evac"], N_WIN)
                        else:
                            pe.wait_ge(sem["mk_ready"], m - 3)
                        project(k, bank[m % 4], mem_hi, mem_lo, TP)
                        return
                    half, c = divmod(k - K_MEMV, 4)
                    if c == 0:
                        pe.wait_ge(sem["mk_ready"], (6, 8)[half])
                    pe.wait_ge(lo_ready, k + 1)
                    wh, wl = parts(k)
                    for u in range(2):
                        b = 2 * c + u
                        for m in range(2):
                            out, rows = bank[2 * half + m][:], slice(P * m, P * m + P)
                            cols = slice(512 * u, 512 * u + 512)
                            pe.matmul(out, mem_hi[:, b, rows], wh[:, cols], start=b == 0, stop=False)
                            pe.matmul(out, mem_lo[:, b, rows], wh[:, cols], start=False, stop=False)
                            ins = pe.matmul(out, mem_hi[:, b, rows], wl[:, cols], start=False, stop=b == KB - 1)
                    ins.then_inc(sem["chunk_used"], 1)

                pe.wait_ge(sem["bsum_ready"], 1)
                for c in range(2):
                    ins = pe.transpose(bank[4][:, 8 * c:8 * c + 8], bsum[:, P * c:P * c + P], cc("ident", 0, 8, rows=slice(0, 8)))
                ins.then_inc(sem["bs_done"], 1)
                for i in range(4):
                    if i == 3:
                        pe.wait_ge(sem["bs_ready"], 1)
                    if i == 1:
                        pe.wait_ge(sem["lp_dve"], 2)
                    for q in range(2):
                        sel = cc("ident", 2 * i + q, 2 * i + q + 1, rows=slice(0, 8)).to_broadcast([8, 64])
                        ins = pe.matmul(bank[(5, 6, 7, 4)[i]][64 * q:64 * q + 64, 0:T], sel, dt8[:], start=True, stop=True)
                    ins.then_inc(sem["dtb_done"], 1)
                fill(K_MEMK)
                pe.wait_ge(sem["xs_ready"], 8)
                pe.wait_ge(sem["xdt_ready"], 1)
                for g in range(2):
                    for c in range(2):
                        a = 256 * c + P * g
                        ins = pe.transpose(bank[5][:, a:a + P], xc[:, 4 + g, P * c:P * c + P], ident)
                ins.then_inc(sem["btok_done"], 1)
                pe.wait_ge(sem["xdt_ready"], 4)
                for c in range(2):
                    for i in range(4):
                        ins = pe.transpose(bank[6 + c][:, P * i:P * i + P], xdt[:, i, P * c:P * c + P], ident)
                    ins.then_inc(sem["xtok_done"], 1)
                for g in range(2):
                    if g == 1:
                        pe.wait_ge(sem["btok_ready"], 1)
                    for c in range(2):
                        ins = pe.matmul(bank[4 + g][:, 256 * c:256 + P * c], xc[:, 4 + g, P * c:P * c + P], xc[:, 6 + g, P * c:TP], start=True, stop=True)
                    ins.then_inc(sem["g_done"], 1)
                fill(K_MEMK + 1)

                def sums(h):
                    if h < 2:
                        pe.wait_ge(sem["xtok_ready"], h + 1)
                    else:
                        pe.wait_ge(sem["d_ready"], h - 1)
                    sel = cc("ident", h, h + 1, rows=slice(0, 8)).to_broadcast([8, P])
                    pe.matmul(bank[6 + h % 2][:, 0:T], sel, bsum[:], start=True, stop=True).then_inc(sem["bc_done"], 1)

                def head(out, lhs, matrix, done):
                    pe.matmul(out, lhs[0], matrix[:, 0:TP], start=True, stop=False, skip_group_check=True)
                    pe.matmul(out[:, P:TP], lhs[1], matrix[:, TP:384], start=False, stop=True, skip_group_check=True).then_inc(sem[done], 1)

                def ssd_head(h):
                    i = h // 2
                    pe.wait_ge(sem["m_ready"], h + 1)
                    if h % 2 == 0:
                        pe.wait_ge(sem["gm_ready"], 2)
                        if i >= 2:
                            pe.wait_ge(sem["y_evac"], i - 1)
                    q = 64 * (h % 2)
                    head(bank[4 + i % 2][q:q + 64, 0:TP], [xtok[:, c, 64 * h:64 * h + 64] for c in range(2)], mbuf[:, h % 2, :], "y_done")

                sums(0)
                sums(1)
                fill(K_MEMK + 2)
                for i in range(4):
                    for q in range(2):
                        h = 2 * i + q
                        ssd_head(h)
                        if h + 2 < HEADS_S:
                            sums(h + 2)
                    if i < 3:
                        fill(K_MEMK + 3 + i)
                pe.wait_ge(sem["m_ready"], 8)
                for g in range(2):
                    for c in range(2):
                        ins = pe.matmul(bank[6][:, 256 * g:256 * g + 256], btok[:, c, P * g:P * g + P], xtail[:, c, 256 * g:256 * g + 256],
                                        start=c == 0, stop=c == 1)
                ins.then_inc(sem["ssdp_done"], 1)
                fill(K_MEMK + 6)

                def spread(i):
                    pe.wait_ge(sem["xe_ready"], i + 1)
                    if i == 0:
                        pe.wait_ge(sem["ssdp_ready"], 1)
                    else:
                        pe.wait_ge(sem["xb_evac"], i)
                    for q in range(2):
                        ins = pe.matmul(bank[6 + q][:], ones, xe[:, 4 * q:4 * q + 4, :].rearrange("p b n -> p (b n)"), start=True, stop=True)
                    ins.then_inc(sem["xb_done"], 1)

                def sample_out(i):
                    pe.wait_ge(sem["sst_ready"], i + 1)
                    if i == 0:
                        pe.wait_ge(sem["y_evac"], 4)
                    for b in range(NS):
                        ins = pe.matmul(bank[4][:, NS * i + b:NS * i + b + 1], sst[:, i, b, :], xc[:, 6 + i // 2, TP + b:TP + b + 1], start=True, stop=True)
                    return ins

                spread(0)
                fill(K_MEMK + 7)
                spread(1)
                sample_out(0)
                fill(K_MEMV)
                spread(2)
                sample_out(1)
                spread(3)
                sample_out(2)
                fill(K_MEMV + 1)
                sample_out(3).then_inc(sem["o_done"], 1)
                pe.wait_ge(sem["ssd_sq"], 1)
                pe.wait_ge(sem["xb_evac"], 4)
                for g in range(2):
                    for i in range(2):
                        ins = pe.matmul(bank[6 + g][:, 0:T], ones, sq4[:, 2 * g + i, :], start=i == 0, stop=i == 1)
                    ins.then_inc(sem["sg_done"], 1)
                for kind in range(2):
                    for c in range(2):
                        for i in range(2):
                            a = 256 * c + P * i
                            ins = pe.transpose(bank[5 - kind][:, a:a + P], qkv[:, (2, 8)[kind] + i, P * c:P * c + P], ident)
                    ins.then_inc(sem["vt_done"], 1)
                fill(K_MEMV + 2)
                pe.wait_ge(sem["rkt_ready"], 1)
                pe.wait_ge(sem["vt_ready"], 2)
                for j in range(2):
                    for c in range(2):
                        a = 256 * j + P * c
                        ins = pe.transpose(bank[4][:, a:a + P], gtmp[:, 256 * j + P * c:256 * j + P * c + P], ident)
                ins.then_inc(sem["rkt_done"], 1)
                pe.wait_ge(sem["ke_ready"], 1)
                pe.wait_ge(sem["sg_r"], 2)
                for c in range(2):
                    ins = pe.transpose(bank[7][:, P * c:P * c + P], ke[:, 8, P * c:P * c + P], ident)
                ins.then_inc(sem["gkt_done"], 1)

                pe.wait_ge(sem["rktok_ready"], 1)
                n = 0
                for h in range(HEADS):
                    rows = slice(32 * h, 32 * h + 32)
                    for r in range(5):
                        out = bank[4 + n % 2]
                        if n >= 2:
                            pe.wait_ge(sem["lv_evac"], n - 1)
                        if r == 4:
                            ins = pe.matmul(out[:, 0:P], ke[rows, 0, 0:P], qe[rows, 0, P:TP], start=True, stop=True)
                        else:
                            for l in range(2):
                                for c in range(2):
                                    a, t = 256 * l + P * c, slice(P * c, P * c + P)
                                    if 2 * r + l < 7:
                                        kk, qq = ke[rows, 2 * r + l + 1, t], qe[rows, 2 * r + l + 1, t]
                                    else:
                                        kk, qq = qkv[rows, 1, t], qkv[rows, 0, t]
                                    ins = pe.matmul(out[:, a:a + P], kk, qq, start=True, stop=True)
                        ins.then_inc(sem["lv_done"], 1)
                        n += 1
                    if h == 0:
                        pe.wait_ge(sem["gkt_ready"], 1)
                        for c in range(2):
                            ins = pe.matmul(bank[7][:, 0:TP], gktok[:, c, :], gvtok[:, c, :], start=c == 0, stop=c == 1)
                        ins.then_inc(sem["gs_done"], 1)
                    fill(K_MEMV + 3 + h)
                    pe.wait_ge(sem["mg_ready"], h + 1)
                    q, i = 64 * (h % 2), h // 2
                    head(bank[6][q:q + 64, TP * i:TP * i + TP], [gvtok[:, c, 64 * h:64 * h + 64] for c in range(2)], mg[:, h % 2, :], "gy_done")

                def ret_scores(h):
                    rows = slice(32 * h, 32 * h + 32)
                    if h < 2:
                        pe.wait_ge(sem["lv_evac"], 20)
                    else:
                        pe.wait_ge(sem["mr_ready"], h - 1)
                    for c in range(2):
                        for j in range(2):
                            ins = pe.matmul(bank[4 + h % 2][:, 256 * c:256 + P * c], qkv[rows, 6 + j, P * c:P * c + P], qkv[rows, 4 + j, P * c:TP],
                                            start=j == 0, stop=j == 1)
                    ins.then_inc(sem["rsc_done"], 1)

                ret_scores(0)
                ret_scores(1)
                fill(K_MEMV + 7)
                pe.wait_ge(sem["gs_ready"], 4)
                for h in range(HEADS):
                    pe.wait_ge(sem["mr_ready"], h + 1)
                    q, i = 64 * (h % 2), h // 2
                    head(bank[7][q:q + 64, TP * i:TP * i + TP], [rvtok[:, c, 64 * h:64 * h + 64] for c in range(2)], mg[:, h % 2, :], "ry_done")
                    if h + 2 < HEADS:
                        ret_scores(h + 2)
                pe.wait_ge(sem["gy_evac"], 1)
                for j in range(2):
                    for c in range(2):
                        ins = pe.matmul(bank[6][:, TP * j:TP * j + TP], rktok[:, j, c, :], rvtok[:, c, :], start=c == 0, stop=c == 1)
                ins.then_inc(sem["rs_done"], 1)

                for kind in range(2):
                    pe.wait_ge(sem["xg_ready"], 2 * kind + 2)
                    pe.wait_ge(sem["mr_ready"], 4)
                    if kind:
                        pe.wait_ge(sem["gs_ready"], 12)
                    for i in range(2):
                        ins = pe.matmul(bank[4 + 2 * kind][:], cc("vsel", P * i, P * i + P), xg[:, i, :, :].rearrange("p b n -> p (b n)"), start=i == 0, stop=i == 1)
                    ins.then_inc(sem["vb_done"], 1)
                for kind in range(2):
                    pe.wait_ge(sem["gst_ready"], 1 + 2 * kind)
                    pe.wait_ge(sem["qx_ready"], 1 + 2 * kind)
                    out = bank[5 + 2 * kind]
                    if kind:
                        pe.wait_ge(sem["ry_evac"], 1)
                    for b in range(NS):
                        for q in range(2):
                            for j in range(1 + kind):
                                s_b = gst[:, b, :] if kind == 0 else rst[:, j, b, :]
                                ins = pe.matmul(out[64 * q:64 * q + 64, b:b + NS + 1:NS], s_b, qx[:, kind + j, b, q:4:2], start=j == 0, stop=j == kind)
                    ins.then_inc(sem["go_done"], 1)
                pe.wait_ge(sem["ry_evac"], 3)
                for i in range(2):
                    pe.matmul(bank[6 + i][:, 0:T], cc("bones"), yb[:, 2 + i, :], start=True, stop=True).then_inc(sem["mu_done"], 1)
                pe.wait_ge(sem["gsq_ready"], 1)
                for i in range(2):
                    pe.matmul(bank[4 + i][:, 0:T], cc("bones"), sq4[:, i, :], start=True, stop=True).then_inc(sem["gms_done"], 1)
                pe.wait_ge(sem["gsq_ready"], 2)
                for i in range(2):
                    pe.wait_ge(sem["gms_r"], i + 1)
                    pe.matmul(bank[4 + i][:, 0:T], cc("bones"), sq4[:, 2 + i, :], start=True, stop=True).then_inc(sem["gms_done"], 1)

                pe.wait_ge(sem["mv_ready"], 4)
                pe.wait_ge(sem["y_lo"], KB)
                for m in range(KB):
                    if m >= 4:
                        pe.wait_ge(sem["x_done"], 16 + m - 3)
                    project(K_WOUT + m, bank[m % 4], xn_hi, xn_lo)

                token_sums(2)
                pe.wait_ge(sem["xn_lo"], 3 * KB)
                for m in range(KB):
                    if m < 4:
                        pe.wait_ge(sem["x_done"], 24)
                    else:
                        pe.wait_ge(sem["q_ready"], m - 3)
                    project(K_Q + m, bank[m % 4], xn_hi, xn_lo)
                pe.wait_ge(sem["q_ready"], KB)
                pe.wait_ge(sem["ktv_in"], 32)

                def scores(h):
                    if h >= 2:
                        pe.wait_ge(sem["p_ready"], 2 * h - 2)
                    for c in range(2):
                        for i in range(2):
                            ins = pe.matmul(bank[h % 2][:, TP * c:TP * c + TP], qt[:, 2 * h + i, P * c:P * c + P], kt[:, 2 * h + i, :], start=i == 0, stop=i == 1)
                    ins.then_inc(sem["sc_done"], 1)

                def probs(h):
                    pe.wait_ge(sem["pn_ready"], 2 * h + 2)
                    if h >= 2:
                        pe.wait_ge(sem["prt_ready"], h - 1)
                    for m in range(2):
                        for c in range(2):
                            a = TP * m + P * c
                            ins = pe.transpose(bank[2 + h % 2][:, a:a + P], pr[:, h % 2, c, P * m:P * m + P], ident)
                    ins.then_inc(sem["pt_done"], 1)

                def values(h):
                    pe.wait_ge(sem["prt_ready"], h + 1)
                    if h >= 2:
                        pe.wait_ge(sem["o_lo"], 2 * h - 2)
                    for i in range(2):
                        for m in range(2):
                            a = 256 * h + P * i
                            ins = pe.matmul(bank[4 + h % 2][:, TP * i:TP * i + TP], vt[:, m, a:a + P], prt[:, h % 2, m, :], start=m == 0, stop=m == 1)
                    ins.then_inc(sem["pv_done"], 1)

                def one_row(i, entry, row):
                    a = 32 * entry + 31 - row
                    return apart[i][:, a:a + 32]

                def sample_scores(b):
                    pe.wait_ge(sem[f"kv_in{b % 4}"], 16 * (b // 4 + 1))
                    if b == 0:
                        pe.wait_ge(sem["ss_q"], 2)
                    for d in range(KB):
                        ins = pe.matmul(bank[6][0:32, 0:TP], one_row(d // 4, NS * (d % 4) + b, HEADS * b + d // 2), kv[b % 4][:, TP * d:TP * d + TP],
                                        start=b == 0 and d == 0, stop=b == NS - 1 and d == KB - 1)
                    ins.then_inc(sem["kv_used"], 1)

                scores(0)
                scores(1)
                sample_scores(0)
                sample_scores(1)
                for h in range(HEADS):
                    probs(h)
                    if h + 2 < HEADS:
                        scores(h + 2)
                    if h < 3:
                        sample_scores(2 * h + 2)
                        sample_scores(2 * h + 3)
                    values(h)
                pe.wait_ge(sem["ss_pn"], 1)
                for m in range(2):
                    ins = pe.transpose(bank[7][:, 32 * m:32 * m + 32], ps_s[:, P * m:P * m + P], cc("ident", 0, 32, rows=slice(0, 32)))
                ins.then_inc(sem["ss_t2"], 1)
                pe.wait_ge(sem["ss_pts"], 1)
                for b in range(NS):
                    n = NS + b
                    pe.wait_ge(sem[f"kv_in{n % 4}"], 16 * (n // 4 + 1))
                    for h in range(HEADS):
                        for m in range(2):
                            r = HEADS * b + h
                            ins = pe.matmul(bank[6][0:32, 0:TP], one_row(m, r, r), kv[n % 4][:, D * m + TP * h:D * m + TP * h + TP],
                                            start=r == 0 and m == 0, stop=r == HEADS * NS - 1 and m == 1)
                    ins.then_inc(sem["kv_used"], 1)
                pe.wait_ge(sem["ss_o"], 1)
                for i in range(2):
                    ins = pe.transpose(bank[7][:, 64 + 32 * i:96 + 32 * i], os_s[:, P * i:P * i + P], cc("ident", 0, 32, rows=slice(0, 32)))
                ins.then_inc(sem["ss_t3"], 1)
                pe.wait_ge(sem["o_lo"], KB + 2)
                for m in range(KB):
                    if m >= 4:
                        pe.wait_ge(sem["x_done"], 24 + m - 3)
                    project(K_O + m, bank[m % 4], xn_hi, xn_lo)

                ffn(1)
                layer_end(pe, "pe")

            token_sums(0)


PAST = 2048


def build_consts():
    c = np.zeros((P, NCST), np.float64)

    def put(name, a, rows=slice(0, P)):
        lo, hi = CST[name]
        c[rows, lo:hi] = a

    i = np.arange(P)
    put("ident", np.eye(P))
    put("ones", 1.0)
    upper = (i[:, None] <= i[None, :]).astype(np.float64)
    put("tri", np.concatenate([upper, np.ones((P, P)), upper], 1))
    pos = np.concatenate([np.arange(TP), np.full(NS, PAST)]).astype(np.float32)
    inv = (np.float32(10000.0) ** (-np.arange(32, dtype=np.float32) / np.float32(32))).astype(np.float32)
    ang = (pos[None, :] * inv[i % 32][:, None]).astype(np.float32).astype(np.float64)
    put("cos", np.cos(ang))
    put("sin", np.sin(ang))
    lg = np.log1p(-np.exp2(-5.0 - np.arange(HEADS)))
    dist = np.concatenate([np.arange(TP)[None, :] - i[:, None], i[None, :] - i[:, None]], 1)
    dec = [np.where(dist >= 0, np.exp(lg[h] * np.maximum(dist, 0)), 0.0) / 8 for h in range(HEADS)]
    put("decay", np.concatenate(dec, 1))
    head = i // 32
    put("rtail", np.exp(lg[head][:, None] * (TP - 1 - np.arange(TP))[None, :]) / 8)
    put("gamma", np.exp(lg[head])[:, None])
    masks = []
    for span in LEVELS[1:]:
        s, t = i[:, None], i[None, :]
        masks.append((s // (2 * span) == t // (2 * span)) & (s // span % 2 == 0) & (t // span % 2 == 1))
    masks.append(i[:, None] == i[None, :])
    put("lmask", np.concatenate(masks, 1))
    put("bones", (i[:, None] // 64 == i[None, :] // 64) / 64.0)
    put("vsel", np.concatenate([(2 * b + i[:, None] // 64 == head[None, :]) for b in range(2)], 1))
    put("hmask", head[:, None] == np.arange(4)[None, :])
    put("id64", i[:, None] % 64 == np.arange(64)[None, :])
    put("eps", EPS)
    return c.astype(np.float32)


def blocks(v):
    return np.swapaxes(v.reshape(v.shape[:-1] + (-1, P)), -1, -2)


def chunks_by_block(w):
    n, k, m = w.shape
    return w.reshape(n, k // P, P, m // P, P).transpose(0, 3, 2, 1, 4).reshape(n, m // P, P, k)


def lay_out(inputs):
    g = {k: np.asarray(v) for k, v in inputs.items()}
    depth = g["w_in"].shape[0]
    win = g["w_in"]
    z, xbc, dt, gq, gk, gv, gg, glr, rq, rk, rv, rg = np.split(
        win, np.cumsum([512, 1024, 8, 128, 128, 256, 256, 16, 256, 256, 256]), axis=2)

    def halves(w):
        return w.reshape(depth, D, HEADS, 2, 32).transpose(0, 1, 3, 2, 4).reshape(depth, D, 256)

    mixed = np.concatenate([xbc, z, gq, gk, gv, halves(rq), halves(rk), rv, gg, rg], axis=2)

    def ffn_chunks(up, down):
        u = chunks_by_block(up)
        gate, up_ = u[:, :2 * HALF], u[:, 2 * HALF:]
        pairs = np.stack([gate, up_], 2).reshape(depth, 2, 2 * HALF, P, CH)
        dn = down.reshape(depth, 2, HALF, P, KB, P).transpose(0, 1, 4, 2, 3, 5)
        dn = dn.reshape(depth, 2, HALF, TILES, P, P).transpose(0, 1, 2, 4, 3, 5).reshape(depth, 2, HALF, P, CH)
        return np.concatenate([pairs, dn], 2).reshape(depth, 2 * HALF_CH, P, CH)

    mv = g["xattn_w_v"].reshape(depth, 4, 2, P, 2, 512).transpose(0, 4, 1, 3, 2, 5).reshape(depth, 8, P, CH)
    w = np.concatenate([ffn_chunks(g["ffn1_w_up"], g["ffn1_w_down"]), chunks_by_block(mixed), chunks_by_block(g["xattn_w_k"]), mv,
                        chunks_by_block(g["w_out"]), chunks_by_block(g["xattn_w_q"]), chunks_by_block(g["xattn_w_o"]),
                        ffn_chunks(g["ffn2_w_up"], g["ffn2_w_down"])], 1)
    w = w.reshape(depth * NCH, P, CH)
    w = np.concatenate([w, w[:RAW]], 0)

    p = np.zeros((depth + 1, P, NPAR), np.float32)

    def put(name, a, rows=slice(0, P)):
        lo, hi = PAR[name]
        p[:depth, rows, lo:lo + a.shape[-1]] = a

    for name, key in (("n1", "norm_ffn1"), ("n2", "norm_mix"), ("n3", "norm_xattn"), ("n4", "norm_ffn2"), ("cb", "conv_b"),
                      ("ssdw", "ssd_norm_w"), ("glaw", "gla_norm_w"), ("retw", "ret_norm_w"), ("glab", "gla_b_gate")):
        put(name, blocks(g[key]))
    put("cw", g["conv_w"].reshape(depth, 4, 8, P).transpose(0, 3, 2, 1).reshape(depth, P, 32))
    small = np.zeros((depth, D, SM), np.float32)
    small[:, :, 0:8], small[:, :, 32:48] = dt, glr
    put("ws", small.reshape(depth, KB, P, SM).transpose(0, 2, 1, 3).reshape(depth, P, KB * SM))
    put("gwg", g["gla_w_gate"], slice(32, 48))
    put("dtb", g["dt_bias"][:, :, None], slice(0, 8))
    put("alog", g["a_log"][:, :, None], slice(0, 8))
    put("dsk", np.repeat(g["d_skip"].reshape(depth, 4, 2), 64, axis=2).transpose(0, 2, 1))
    lo, hi = PAR["n1"]
    p[depth, :, lo:hi] = blocks(g["final_norm_w"])

    tokens = np.concatenate([g["x_prompt"][0], g["x_sample"][:, 0]], 0)
    x = tokens.T.reshape(KB, P, T).transpose(1, 0, 2)
    mem = g["mem_prompt"][0].T.reshape(KB, P, TP).transpose(1, 0, 2)
    ck = g["cache_mem_k"].reshape(depth, NS, TP, KB, P).transpose(0, 1, 4, 3, 2).reshape(depth * NS, P, KB * TP)
    cv = g["cache_mem_v"].reshape(depth, NS, 2, P, D).transpose(0, 1, 3, 2, 4).reshape(depth * NS, P, 2 * D)
    ssd = g["state_ssd"].reshape(depth, NS, 4, 2, P, 64).transpose(0, 4, 2, 1, 3, 5).reshape(depth, P, 4 * NS * P)
    conv = g["state_ssd_conv"].reshape(depth, NS, 3, 8, P).transpose(0, 4, 3, 1, 2).reshape(depth, P, 8 * NS * 3)
    gla = g["state_gla"].reshape(depth, NS, P, 64).transpose(0, 2, 1, 3).reshape(depth, P, NS * 64)
    ret = g["state_ret"].reshape(depth, NS, HEADS, 2, 32, 64).transpose(0, 2, 4, 3, 1, 5).reshape(depth, P, 2 * NS * 64)
    return depth, [("wts", w), ("params", p), ("consts", build_consts()), ("x_in", x), ("mem_in", mem), ("ck", ck), ("cv", cv),
                   ("st_ssd", ssd), ("st_conv", conv), ("st_gla", gla), ("st_ret", ret)]


def kernel(**inputs):
    import concourse.bacc as bacc
    from concourse.bass_utils import run_bass_kernel_spmd as run

    depth, arrays = lay_out(inputs)
    nc = bacc.Bacc("TRN2", target_bir_lowering=False, num_devices=1)
    feed, args = {}, []
    for name, a in arrays:
        feed[f"in_{name}"] = np.ascontiguousarray(a)
        args.append(nc.dram_tensor(f"in_{name}", a.shape, F32, kind="ExternalInput").ap())
    outs = [("y", (P, KB, T)), ("conv", (depth, P, 8 * 9 * 3)), ("ssdp", (depth, P, 512)), ("grp", (depth, P, 192)),
            ("mk", (depth * KB, P, TP)), ("mv", (depth, P, 2, D)), ("ssds", (depth, P, 4 * NS * P)), ("glas", (depth, P, NS * 64)),
            ("rets", (depth, P, 2 * NS * 64))]
    for name, shape in outs:
        args.append(nc.dram_tensor(f"out_{name}", shape, F32, kind="ExternalOutput").ap())
    build(nc, depth, *args)
    r = run(nc, [feed], core_ids=[0]).results[0]
    o = {name: np.asarray(r[f"out_{name}"]).reshape(shape) for name, shape in outs}

    y = o["y"].transpose(2, 1, 0).reshape(T, D)
    conv = o["conv"].reshape(depth, P, 8, 9, 3).transpose(0, 3, 4, 2, 1).reshape(depth, 9, 3, 1024)
    ssd_p = o["ssdp"].reshape(depth, P, 8, 64).transpose(0, 2, 1, 3)[:, None]
    grp = o["grp"].reshape(depth, HEADS, 32, 3, 64)
    gla_p = grp[:, None, :, :, 0]
    ret_p = grp[:, :, :, 1:].transpose(0, 1, 3, 2, 4).reshape(depth, 1, HEADS, 64, 64)
    mk = o["mk"].reshape(depth, D, TP).transpose(0, 2, 1).reshape(depth, 1, TP, 4, 256)
    mv = o["mv"].transpose(0, 2, 1, 3).reshape(depth, 1, TP, 4, 256)
    ssd_s = o["ssds"].reshape(depth, P, 4, NS, 2, 64).transpose(0, 3, 2, 4, 1, 5).reshape(depth, NS, 8, P, 64)
    gla_s = o["glas"].reshape(depth, HEADS, 32, NS, 64).transpose(0, 3, 1, 2, 4)
    ret_s = o["rets"].reshape(depth, HEADS, 32, 2, NS, 64).transpose(0, 4, 1, 3, 2, 5).reshape(depth, NS, HEADS, 64, 64)
    c = np.ascontiguousarray
    return (c(y[None, :TP]), c(y[TP:, None]), c(ssd_p), c(conv[:, None, 0]), c(gla_p), c(ret_p), c(mk), c(mv),
            c(ssd_s), c(conv[:, 1:]), c(gla_s), c(ret_s))
```

```python
from contextlib import ExitStack

import numpy as np

import concourse.bass as bass
from concourse import mybir

F32 = mybir.dt.float32
F32R = mybir.dt.float32r
ALU = mybir.AluOpType
ACT = mybir.ActivationFunctionType
AX = mybir.AxisListType

P = 128
D = 1024
KB = D // P
TP, NS = 256, 8
T = TP + NS
FF = 2816
HALF = FF // P // 2
EPS = 1e-6

TILES = 8
CH = TILES * P
RAW, SPL = 11, 3
HALF_CH = 3 * HALF
K_FFN1 = 0
K_WIN = K_FFN1 + 2 * HALF_CH
N_WIN = 26
K_MEMK = K_WIN + N_WIN
K_MEMV = K_MEMK + 8
K_WOUT = K_MEMV + 8
K_Q = K_WOUT + 8
K_O = K_Q + 8
K_FFN2 = K_O + 8
NCH = K_FFN2 + 2 * HALF_CH
assert NCH % (RAW * SPL) == 0 and K_FFN2 % (RAW * SPL) == 0

OUT = [(range(2 * c, 2 * c + 2), range(0, 4)) for c in range(4)] + [(range(4 * c, 4 * c + 4), range(4 + 2 * g, 6 + 2 * g)) for g in range(2) for c in range(2)]
OUT_AT = [8 * (c // 4) + (2 * c if c < 4 else 4 * (c - 4)) for c in range(8)]

HEADS_S, HEADS = 8, 4
SM = 48
PADW = TP + 3 + 4 * NS
LEVELS = [128, 64, 32, 16, 8, 4, 2, 1]

B_Z, B_GQ, B_GK, B_GV, B_RQ, B_RK, B_RV, B_GG = 8, 12, 13, 14, 16, 18, 20, 22


def columns(*fields):
    at, where = 0, {}
    for name, width in fields:
        where[name] = (at, at + width)
        at += width
    return where, at


PAR, NPAR = columns(("n1", 8), ("n2", 8), ("n3", 8), ("n4", 8), ("cw", 32), ("cb", 8), ("ws", 8 * SM + 80),
                    ("gwg", 128), ("dtb", 1), ("alog", 1), ("dsk", 4), ("ssdw", 4), ("glaw", 2), ("retw", 2),
                    ("glab", 1))
CST, NCST = columns(("ident", 128), ("ones", 128), ("eps", 1), ("zero", 1), ("tri", 384), ("cos", T), ("sin", T), ("decay", 4 * 384),
                    ("rtail", 256), ("gamma", 1), ("lmask", 8 * 128), ("bones", 128), ("vsel", 256), ("hmask", 4),
                    ("id64", 64))
CST_FIRST = CST["tri"][0]


def build(nc, depth, wts, params, consts, x_in, mem_in, ck, cv, st_ssd, st_conv, st_gla, st_ret,
          y_out, o_conv, o_ssdp, o_grp, o_mk, o_mv, o_ssds, o_glas, o_rets):
    with ExitStack() as ctx:
        base = (nc.sbuf_base + 63) // 64 * 64
        room = (nc.sbuf_usable_end - base - 128) // 64 * 64
        ctx.enter_context(nc.sbuf_tensor("arena", [P, room // 4], F32))
        top = [base]
        sizes = {F32: 4, F32R: 4}

        def place(name, shape, dt=F32, at=None):
            off = top[0] if at is None else at
            n = 4 * int(np.prod(shape[1:]))
            if at is None:
                top[0] += (n + 31) // 32 * 32
            assert off + n <= base + room, (name, off + n - base - room)
            return nc.alloc_sbuf_tensor_at(name, list(shape), dt, offset=off)

        raw = place("raw", [P, RAW, CH])
        w_hi = place("w_hi", [P, SPL, CH], F32R)
        w_lo = place("w_lo", [P, SPL, CH], F32R)
        x = place("x", [P, KB, T])
        xn_at = top[0]
        xn_hi = place("xn_hi", [P, KB, T], F32R)
        xn_lo = place("xn_lo", [P, KB, T], F32R)
        h_at = top[0]
        h_hi = place("h_hi", [P, HALF, T], F32R)
        h_lo = place("h_lo", [P, HALF, T], F32R)
        mem_hi = place("mem_hi", [P, KB, TP], F32R)
        mem_raw = place("mem_raw", [P, KB, TP], at=top[0])
        mem_lo = place("mem_lo", [P, KB, TP], F32R)
        par = place("par", [P, NPAR])
        cst = place("cst", [P, NCST])
        r_bc = place("r_bc", [P, T])
        mix_at = top[0]

        sq = place("sq", [P, KB, T])
        gbuf = place("gbuf", [P, 2, T], at=mix_at + 8448)
        ubuf = place("ubuf", [P, 2, T], at=mix_at + 8448 + 2112)
        sbuf_ = place("sbuf", [P, 2, T], at=mix_at + 8448 + 4224)
        h32 = place("h32", [P, 2, T], at=mix_at + 8448 + 6336)
        yo = place("yo", [P, KB, T], at=mix_at + 16896)

        top[0] = mix_at
        xc = place("xc", [P, 8, T])
        yg = place("yg", [P, 8, T])
        qkv = place("qkv", [P, 10, T])
        bsum = place("bsum", [8, T])
        glog = place("glog", [P, T])
        kst = place("kst", [P, 2, TP])
        vst = place("vst", [P, 2, 512])
        convst = place("convst", [P, 8, 9, 3])
        convld = place("convld", [P, 8, NS, 3])
        gst = place("gst", [P, NS, 64])
        rst = place("rst", [P, 2, NS, 64])
        tmp_at = top[0]
        cbuf = place("cbuf", [P, 2, 288], at=tmp_at)
        sm = place("sm", [SM, T], at=tmp_at + 2304)
        sp = [place(f"sp{i}", [P, T], at=tmp_at + 3360 + 1056 * i) for i in range(3)]
        xp = place("xp", [P, 8, PADW], at=h_at)
        ws_hi = place("ws_hi", [P, 8 * SM + 80], F32R, at=h_at + 9344)
        ws_lo = place("ws_lo", [P, 8 * SM + 80], F32R, at=h_at + 9344 + 1856)
        dt8 = place("dt8", [8, T], at=h_at + 13056)
        na8 = place("na8", [8, 1], at=h_at + 14112)
        la8 = place("la8", [8, T], at=h_at + 14144)
        e8 = place("e8", [8, T], at=h_at + 19456)
        rp = [place(f"rp{i}", [P, 2, T], at=h_at + 15232 + 2112 * i) for i in range(2)]
        bs = place("bs", [P, 2, 8])
        dec = place("dec", [P, 8, NS])
        xdt = place("xdt", [P, 4, T])
        gm = place("gm", [P, 2, 384])
        dbuf = place("dbuf", [P, 2, 392])
        sq_s = place("sq_s", [P, 4, T], at=tmp_at + 320)
        rn_s = place("rn_s", [P, 2, T], at=tmp_at + 5120)
        xtok = place("xtok", [P, 2, 512], at=h_at)
        btok = place("btok", [P, 2, 256], at=h_at + 4096)
        xtail = place("xtail", [P, 2, 512], at=h_at + 6144)
        mbuf = place("mbuf", [P, 2, 384], at=h_at + 10240)
        xe = place("xe", [P, NS, P], at=h_at + 13312)
        tb = place("tb", [P, NS, P], at=h_at)
        ssdo = place("ssdo", [P, 512], at=h_at + 21184)
        sst = place("sst", [P, 4, NS, P], at=xn_at)
        ke = place("ke", [P, 9, TP], at=h_at)
        qe = place("qe", [P, 8, TP], at=h_at + 9216)
        gvtok = place("gvtok", [P, 2, TP], at=h_at + 17408)
        rvtok = place("rvtok", [P, 2, TP], at=h_at + 19456)
        gktok = place("gktok", [P, 2, P], at=h_at + 21504)
        mg = place("mg", [P, 2, 384], at=tmp_at)
        gtmp = place("gtmp", [P, 512], at=tmp_at + 3072)
        rktok = place("rktok", [P, 2, 2, P], at=tmp_at + 5120)
        sto = place("sto", [P, 3, 64], at=tmp_at + 7168)
        gdec = place("gdec", [P, NS], at=tmp_at + 7936)
        qx = place("qx", [P, 3, NS, 4], at=tmp_at + 7968)
        yb = place("yb", [P, 4, T], at=tmp_at + 8352)
        xg = place("xg", [P, 2, NS, 64], at=h_at)
        tg = place("tg", [P, NS, 64], at=h_at + 4096)
        sq4 = place("sq4", [P, 4, T], at=h_at + 6144)
        rn = place("rn", [P, 4, T], at=h_at + 10368)
        qt = place("qt", [P, KB, T], at=mix_at)
        kt = place("kt", [P, KB, TP], at=mix_at + 8448)
        vt = place("vt", [P, 2, D], at=mix_at + 16640)
        pr = place("pr", [P, 2, 2, TP], at=mix_at + 24832)
        prt = place("prt", [P, 2, 2, TP], at=mix_at + 28928)
        mx = place("mx", [P, 4, 2], at=mix_at + 33024)
        nmx = place("nmx", [P, 4, 2], at=mix_at + 33056)
        psm = place("psm", [P, 4, 2], at=mix_at + 33088)
        rsm = place("rsm", [P, 4, 2], at=mix_at + 33120)
        ps_s = place("ps_s", [32, TP], at=mix_at + 33408)
        m32 = place("m32", [32, 4], at=mix_at + 34688)
        KV_AT = [h_at, h_at + 8192, mix_at + 34720, mix_at + 42912]
        kv = [place(f"kv{i}", [P, 2048], at=KV_AT[i]) for i in range(4)]
        apart = [place(f"apart{i}", [P, 33 * 32], at=(h_at + 16384, mix_at + 51104)[i]) for i in range(2)]
        os_s = place("os_s", [32, TP], at=mix_at + 55328)

        bank = [ctx.enter_context(nc.psum_tensor(f"bank{i}", [P, 512], F32)) for i in range(8)]

        def pc(name, a=0, b=None, rows=slice(0, P)):
            lo, hi = PAR[name]
            return par[rows, lo + a:hi if b is None else lo + b]

        def cc(name, a=0, b=None, rows=slice(0, P)):
            lo, hi = CST[name]
            return cst[rows, lo + a:hi if b is None else lo + b]

        ident = cc("ident")
        ones = cc("ones")

        def new(name):
            return ctx.enter_context(nc.semaphore(name))

        loaded = new("loaded")
        tables_in = new("tables_in")
        par_landed = new("par_landed")
        landed = [new(f"landed{i}") for i in range(RAW)]
        hi_ready = new("hi_ready")
        lo_ready = new("lo_ready")
        layer_done = new("layer_done")
        go = {n: new(f"go_{n}") for n in ("pe", "act", "dve", "pool")}

        names = """chunk_used xn_hi xn_lo sq_ready ss_ready r_ready x_done g_ready up_evac s_ready h32_ready hhi_ready h_ready
            down_done out_done st_in st_ssd_in win_evac ws_hi_ready ws_ready small_done small_evac gate_done conv_done xs_ready
            conv_out_ready z_ready gg_ready bsum_ready lp_act lp_dve bs_done bs_ready dtb_done xdt_ready btok_done
            btok_ready xtok_done xtok_ready g_done gm_ready bc_done d_ready e_ready m_ready y_done y_evac ssdp_done
            ssdp_ready xe_ready xb_done xb_evac sst_ready o_done ssd_gated ssd_sq sg_done sg_r vt_done vt_ready d9_ready
            e9_ready ke_ready gkt_done gkt_ready rkt_ready rkt_done rktok_ready lv_done lv_evac mg_ready gy_done gy_evac
            gs_done gs_ready rsc_done mr_ready ry_done ry_evac rs_done xg_ready vb_done gdec_ready gst_ready qx_ready
            go_done gsq_ready gms_done gms_r mu_done mk_ready mk_out0 mk_out1 mv_ready mv_out0 mv_out1 y_hi y_lo ssdp_out
            ssds_out q_ready kv_in0 kv_in1 kv_in2 kv_in3 kv_used sc_done mx_ready p_ready pn_ready pt_done prt_ready
            pv_done o_hi o_lo ss_zero ss_q ss_mx ss_p ss_pn ss_t2 ss_pts ss_o ss_t3 act_chain dve_chain mix_out y_final
            ktv_in mem_in mem_hi_ready mem_lo_ready""".split()
        sem = {n: new(n) for n in names}
        first, last = sem[names[0]].num, sem[names[-1]].num
        assert last - first == len(names) - 1

        block = ctx.enter_context(nc.Block())

        X_DONE = [0, 16, 40, 48]

        vg, ng, eg, ug = sp[1], sp[2], rp[0][:, 0, :], rp[1][:, 0, :]

        SUMS = [bank[6], bank[3], bank[6], bank[6]]

        def layer_end(eng, name):
            eng.drain().then_inc(layer_done, 1)
            eng.wait_ge(go[name], 1)
            eng.sem_inc(go[name], -1)

        @block.sync
        def _(sp):
            sp.dma_start(cst[:, 0:CST_FIRST], consts[:, 0:CST_FIRST]).then_inc(loaded, 16)
            sp.dma_start(par[:], params[0]).then_inc(loaded, 16)
            sp.dma_start(x[:], x_in).then_inc(loaded, 16)
            for s in range(RAW):
                sp.dma_start(raw[:, s, :], wts[s]).then_inc(landed[s], 16)
            sp.dma_start(cst[:, CST_FIRST:NCST], consts[:, CST_FIRST:NCST]).then_inc(tables_in, 16)

            with sp.Fori(0, depth) as layer:
                def at_layer(t):
                    return t[bass.ds(layer, 1)]

                def row(t, k):
                    return t[bass.ds(layer * NCH + (k + RAW), 1)].rearrange("a p c -> (a p) c")

                def stream(k):
                    sp.wait_ge(lo_ready, k + 1)
                    sp.dma_start(raw[:, k % RAW, :], row(wts, k)).then_inc(landed[k % RAW], 16)

                def stream_loop(g0, g1):
                    with sp.Fori(g0, g1) as g:
                        for s in range(RAW):
                            sp.wait_ge(lo_ready, g * RAW + (s + 1))
                            sp.dma_start(raw[:, s, :], row(wts, g * RAW + s)).then_inc(landed[s], 16)

                def load(dst, src, name):
                    sp.dma_start(dst, src).then_inc(sem[name], 16)

                def store(dst, src, name):
                    sp.dma_start(dst, src).then_inc(sem[name], 16)

                stream_loop(0, 3)
                load(convld[:].rearrange("p a b c -> p (a b c)"), at_layer(st_conv).rearrange("a p c -> (a p) c"), "st_in")
                load(gst[:].rearrange("p a b -> p (a b)"), at_layer(st_gla).rearrange("a p c -> (a p) c"), "st_in")
                load(rst[:].rearrange("p a b c -> p (a b c)"), at_layer(st_ret).rearrange("a p c -> (a p) c"), "st_in")
                load(mem_raw[:], mem_in, "mem_in")
                stream_loop(3, K_MEMK // RAW)
                for k in range(K_MEMK // RAW * RAW, K_FFN2):
                    stream(k)
                    if k == K_MEMK + 2:
                        sp.wait_ge(sem["chunk_used"], K_MEMK)
                        load(sst[:].rearrange("p a b c -> p (a b c)"), at_layer(st_ssd).rearrange("a p c -> (a p) c"), "st_ssd_in")
                        sp.wait_ge(sem["conv_out_ready"], 2)
                        store(at_layer(o_conv).rearrange("a p c -> (a p) c"), convst[:].rearrange("p a b c -> p (a b c)"), "mix_out")
                    if K_MEMK + 3 <= k < K_MEMK + 11:
                        m = k - K_MEMK - 3
                        sp.wait_ge(sem["mk_ready"], m + 1)
                        store(o_mk[bass.ds(layer * KB + m, 1)].rearrange("a p c -> (a p) c"), kst[:, m % 2, :], f"mk_out{m % 2}")
                    if k in (K_MEMV + 6, K_MEMV + 10):
                        half = (k - K_MEMV - 6) // 4
                        sp.wait_ge(sem["mv_ready"], 2 * (half + 1))
                        store(at_layer(o_mv).rearrange("a p m c -> (a p) m c")[:, :, 512 * half:512 * half + 512], vst[:], f"mv_out{half}")
                    if k == K_MEMK + 5:
                        sp.wait_ge(sem["ssdp_ready"], 1)
                        store(at_layer(o_ssdp).rearrange("a p c -> (a p) c"), ssdo[:], "ssdp_out")
                    if k == K_MEMV:
                        sp.wait_ge(sem["sst_ready"], 4)
                        store(at_layer(o_ssds).rearrange("a p c -> (a p) c"), sst[:].rearrange("p a b c -> p (a b c)"), "ssds_out")
                    if k == K_WOUT + 3:
                        sp.wait_ge(sem["gs_ready"], 12)
                        store(at_layer(o_grp).rearrange("a p c -> (a p) c"), sto[:].rearrange("p a b -> p (a b)"), "mix_out")
                        sp.wait_ge(sem["gst_ready"], 1)
                        store(at_layer(o_glas).rearrange("a p c -> (a p) c"), gst[:].rearrange("p a b -> p (a b)"), "mix_out")
                        sp.wait_ge(sem["gst_ready"], 3)
                        store(at_layer(o_rets).rearrange("a p c -> (a p) c"), rst[:].rearrange("p a b c -> p (a b c)"), "mix_out")
                        sp.wait_ge(sem["y_lo"], 8)
                        sp.wait_ge(sem["mix_out"], 64)
                        for i in range(2):
                            sp.wait_ge(sem[f"mk_out{i}"], 64)
                            sp.wait_ge(sem[f"mv_out{i}"], 16)
                        load(kt[:], o_mk[bass.ds(layer * KB, KB)].rearrange("a p c -> p a c"), "ktv_in")
                        load(vt[:], at_layer(o_mv).rearrange("a p m c -> (a p) m c"), "ktv_in")
                        for n in range(4):
                            load(kv[n][:], ck[bass.ds(layer * NS + n, 1)].rearrange("a p c -> (a p) c"), f"kv_in{n}")
                    if k == K_Q + 4:
                        for n in range(4, 2 * NS):
                            sp.wait_ge(sem["kv_used"], n - 3)
                            src = ck if n < NS else cv
                            load(kv[n % 4][:], src[bass.ds(layer * NS + n % NS, 1)].rearrange("a p c -> (a p) c"), f"kv_in{n % 4}")
                stream_loop(K_FFN2 // RAW, K_FFN2 // RAW + 1)
                sp.wait_ge(sem["xn_lo"], 4 * KB)
                sp.dma_start(par[:], params[bass.ds(layer + 1, 1)].rearrange("a p c -> (a p) c")).then_inc(par_landed, 16)
                stream_loop(K_FFN2 // RAW + 1, NCH // RAW)
                sp.wait_ge(sem["ssdp_out"], 16)
                sp.wait_ge(sem["ssds_out"], 16)
                sp.wait_ge(par_landed, 16)
                sp.sem_inc(par_landed, -16)
                sp.wait_ge(layer_done, 4)
                sp.sem_clear(range(first, last + 1))
                sp.sem_inc(layer_done, -4)
                sp.sem_inc(hi_ready, -NCH)
                sp.sem_inc(lo_ready, -NCH)
                for n in go:
                    sp.sem_inc(go[n], 1)

            for s in range(SPL, RAW):
                sp.wait_ge(landed[s], 16)
            sp.wait_ge(sem["h_ready"], KB)
            sp.dma_start(y_out, yo[:]).then_inc(sem["mix_out"], 16)
            sp.wait_ge(sem["mix_out"], 16)

        @block.gpsimd
        def _(pool):
            def low_part(k, wait):
                pool.wait_ge(hi_ready, wait)
                pool.tensor_tensor(w_lo[:, k % SPL, :], raw[:, k % RAW, :], w_hi[:, k % SPL, :].bitcast(F32),
                                   ALU.subtract).then_inc(lo_ready, 1)

            for k in range(SPL):
                low_part(k, k + 1)
            with pool.Fori(0, depth):
                with pool.Fori(0, NCH // (RAW * SPL)) as g:
                    for j in range(RAW * SPL):
                        low_part(j + SPL, g * (RAW * SPL) + (j + SPL + 1))
                layer_end(pool, "pool")

        @block.scalar
        def _(act):
            chain = [0]

            def link(ins):
                chain[0] += 1
                ins.then_inc(sem["act_chain"], 1)
                act.wait_ge(sem["act_chain"], chain[0])

            def high_part(k, used=None):
                if used is not None:
                    act.wait_ge(sem["chunk_used"], used)
                act.wait_ge(landed[k % RAW], 16)
                act.sem_inc(landed[k % RAW], -16)
                act.activation(w_hi[:, k % SPL, :], raw[:, k % RAW, :], ACT.Copy).then_inc(hi_ready, 1)

            def ahead(k):
                high_part(k + SPL, k + 1)

            def norm_square(n, b):
                if n > 0:
                    act.wait_ge(sem["x_done"], X_DONE[n] - KB + b + 1)
                act.activation(sq[:, b, :], x[:, b, :], ACT.Square).then_inc(sem["sq_ready"], 1)

            def norm_high(n, b):
                act.activation(xn_hi[:, b, :], x[:, b, :], ACT.Copy, scale=pc(f"n{n + 1}", b, b + 1)).then_inc(sem["xn_hi"], 1)

            def norm_scale(n):
                act.wait_ge(sem["ss_ready"], n + 1)
                link(act.activation(r_bc[:], SUMS[n][:, 0:T], ACT.Ln, scale=1.0 / D, bias=cc("eps")))
                act.activation(r_bc[:], r_bc[:], ACT.Exp, scale=-0.5).then_inc(sem["r_ready"], 1)

            def ffn(f):
                k0 = (K_FFN1, K_FFN2)[f]
                norm_scale((0, 3)[f])

                def half_ffn(k, b, blocks_after=None):
                    for j in range(HALF):
                        high_part(2 * j + SPL, k + (2 * j + 1))
                        act.wait_ge(sem["g_ready"], b + (j + 1))
                        act.activation(sbuf_[:, j % 2, :], gbuf[:, j % 2, :], ACT.Silu).then_inc(sem["s_ready"], 1)
                        high_part(2 * j + 1 + SPL, k + (2 * j + 2))
                        act.wait_ge(sem["h32_ready"], b + (j + 1))
                        act.activation(h_hi[:, j, :], h32[:, j % 2, :], ACT.Copy).then_inc(sem["hhi_ready"], 1)
                    for c in range(2 * HALF, HALF_CH):
                        high_part(c + SPL, k + (c + 1))
                        if blocks_after is not None:
                            for m in range(KB):
                                if (HALF * (m + 1) - 1) // TILES == c - 2 * HALF:
                                    norm_square(blocks_after, m)
                                    norm_high(blocks_after, m)

                if f == 0:
                    half_ffn(k0, 0)
                    half_ffn(k0 + HALF_CH, HALF, 1)
                else:
                    with act.Fori(0, 2) as half:
                        half_ffn(half * HALF_CH + k0, half * HALF + 2 * HALF)

            act.wait_ge(loaded, 48)
            for k in range(SPL):
                high_part(k)
            with act.Fori(0, depth):
                chain[0] = 0
                for b in range(KB):
                    norm_square(0, b)
                    norm_high(0, b)
                ffn(0)

                act.activation(ws_hi[:], pc("ws"), ACT.Copy).then_inc(sem["ws_hi_ready"], 1)
                norm_scale(1)
                act.activation(na8[:], pc("alog", rows=slice(0, 8)), ACT.Exp).then_inc(sem["z_ready"], 1)

                def conv_act(n):
                    act.wait_ge(sem["conv_done"], n + 1)
                    act.activation(xc[:, n, 0:TP], cbuf[:, n % 2, 0:TP], ACT.Silu)
                    act.activation(xc[:, n, TP:T], cbuf[:, n % 2, TP + 3:TP + 3 + 29:4], ACT.Silu).then_inc(sem["xs_ready"], 1)

                for n in range(B_GG):
                    ahead(K_WIN + n)
                    if 1 <= n <= 8:
                        conv_act(n - 1)
                    if n == 12:
                        act.wait_ge(sem["win_evac"], 12)
                        act.activation(yg[:, 0:4, :], yg[:, 0:4, :], ACT.Silu).then_inc(sem["z_ready"], 1)
                    if n == 13:
                        act.wait_ge(sem["mem_in"], 16)
                        act.activation(mem_hi[:], mem_raw[:], ACT.Copy).then_inc(sem["mem_hi_ready"], 1)
                    if n == 14:
                        act.wait_ge(sem["lp_dve"], 1)
                        act.activation(e8[:], sp[0][0:8, :], ACT.Exp).then_inc(sem["lp_act"], 1)
                        act.wait_ge(sem["lp_dve"], 2)
                        act.activation(eg, ng[:], ACT.Exp).then_inc(sem["lp_act"], 1)
                    if n == 16:
                        act.wait_ge(sem["lp_dve"], 3)
                        act.activation(e8[:], dt8[:], ACT.Ln).then_inc(sem["lp_act"], 1)
                        act.wait_ge(sem["lp_dve"], 4)
                        act.activation(eg, ug, ACT.Ln).then_inc(sem["lp_act"], 1)
                def fill(k):
                    ahead(k)
                    if k < K_MEMK:
                        return
                    if k < K_MEMV:
                        m = k - K_MEMK
                        if m >= 2:
                            act.wait_ge(sem[f"mk_out{m % 2}"], 16 * (m // 2))
                        act.activation(kst[:, m % 2, :], bank[m % 4][:, 0:TP], ACT.Copy).then_inc(sem["mk_ready"], 1)
                    elif (k - K_MEMV) % 4 == 3:
                        half = (k - K_MEMV) // 4
                        if half:
                            act.wait_ge(sem["mv_out0"], 16)
                        for m in range(2):
                            act.activation(vst[:, m, :], bank[2 * half + m][:], ACT.Copy).then_inc(sem["mv_ready"], 1)

                fill(K_WIN + B_GG)
                act.wait_ge(sem["btok_done"], 1)
                act.activation(btok[:].rearrange("p c n -> p (c n)"), bank[5][:], ACT.Copy).then_inc(sem["btok_ready"], 1)
                for c in range(2):
                    act.wait_ge(sem["xtok_done"], c + 1)
                    act.activation(xtok[:, c, :], bank[6 + c][:], ACT.Copy).then_inc(sem["xtok_ready"], 1)
                fill(K_WIN + B_GG + 1)

                def decays(h):
                    act.wait_ge(sem["d_ready"], h + 1)
                    act.activation(dec[:, h, :], dbuf[:, h % 2, 384:392], ACT.Exp)
                    act.activation(dbuf[:, h % 2, 0:384], dbuf[:, h % 2, 0:384], ACT.Exp).then_inc(sem["e_ready"], 1)

                decays(0)
                decays(1)
                fill(K_WIN + B_GG + 2)
                for h in range(2, HEADS_S):
                    decays(h)
                    if h % 2 == 0:
                        fill(K_WIN + B_GG + 2 + h // 2)
                act.wait_ge(sem["ssdp_done"], 1)
                act.activation(ssdo[:], bank[6][:], ACT.Copy).then_inc(sem["ssdp_ready"], 1)
                act.wait_ge(sem["win_evac"], N_WIN)
                act.activation(yg[:, 4:8, :], yg[:, 4:8, :], ACT.Silu).then_inc(sem["gg_ready"], 1)
                for k in range(K_MEMK + 2, K_MEMK + 7):
                    fill(k)
                act.wait_ge(sem["d9_ready"], 1)
                act.activation(ke[:], ke[:], ACT.Exp).then_inc(sem["e9_ready"], 1)
                act.wait_ge(sem["ssd_gated"], 4)
                act.activation(sq_s[:], yg[:, 0:4, :], ACT.Square).then_inc(sem["ssd_sq"], 1)
                fill(K_MEMK + 7)
                fill(K_MEMV)
                for g in range(2):
                    act.wait_ge(sem["sg_done"], g + 1)
                    ins = act.activation(rn_s[:, g, :], bank[6 + g][:, 0:T], ACT.Ln, scale=1.0 / 256, bias=cc("eps"))
                link(ins)
                act.activation(rn_s[:], rn_s[:], ACT.Exp, scale=-0.5).then_inc(sem["sg_r"], 1)
                act.wait_ge(sem["vt_done"], 1)
                act.activation(gvtok[:].rearrange("p c n -> p (c n)"), bank[5][:], ACT.Copy).then_inc(sem["vt_ready"], 1)
                act.wait_ge(sem["ssdp_out"], 16)
                act.wait_ge(sem["vt_done"], 2)
                act.activation(rvtok[:].rearrange("p c n -> p (c n)"), bank[4][:], ACT.Copy).then_inc(sem["vt_ready"], 1)
                fill(K_MEMV + 1)
                act.wait_ge(sem["y_final"], 4)
                act.activation(gdec[:], glog[:, TP:T], ACT.Exp).then_inc(sem["gdec_ready"], 1)
                act.wait_ge(sem["rkt_done"], 1)
                act.activation(rktok[:].rearrange("p a c n -> p (a c n)"), bank[4][:], ACT.Copy).then_inc(sem["rktok_ready"], 1)
                act.wait_ge(sem["gkt_done"], 1)
                act.activation(gktok[:].rearrange("p c n -> p (c n)"), bank[7][:, 0:TP], ACT.Copy).then_inc(sem["gkt_ready"], 1)
                fill(K_MEMV + 2)
                act.wait_ge(sem["ssds_out"], 16)

                def mixed_high(a, b):
                    act.wait_ge(sem["y_final"], b)
                    for i in range(a, b):
                        act.activation(xn_hi[:, i, :], yg[:, i, :], ACT.Copy).then_inc(sem["y_hi"], 1)

                mixed_high(0, 4)
                for k in range(K_MEMV + 3, K_WOUT + 2):
                    if k < K_WOUT:
                        fill(k)
                    else:
                        ahead(k)

                def head_scale(kind):
                    for i in range(2):
                        act.wait_ge(sem["gms_done"], 2 * kind + i + 1)
                        ins = act.activation(rn[:, 2 * kind + i, :], bank[4 + i][:, 0:T], ACT.Ln, bias=cc("eps"))
                    link(ins)
                    act.activation(rn[:, 2 * kind:2 * kind + 2, :], rn[:, 2 * kind:2 * kind + 2, :], ACT.Exp, scale=-0.5).then_inc(sem["gms_r"], 1)

                act.wait_ge(sem["gy_evac"], 4)
                act.activation(sq4[:, 0:2, :], yb[:, 0:2, :], ACT.Square).then_inc(sem["gsq_ready"], 1)
                head_scale(0)
                act.wait_ge(sem["ry_evac"], 6)
                act.activation(sq4[:, 2:4, :], yb[:, 2:4, :], ACT.Square).then_inc(sem["gsq_ready"], 1)
                ahead(K_WOUT + 2)
                mixed_high(4, 6)
                head_scale(1)

                ahead(K_WOUT + 3)
                mixed_high(6, 8)
                for c in range(4, 8):
                    ahead(K_WOUT + c)
                    if c >= 6:
                        for b in OUT[c][0]:
                            norm_square(2, b)

                for b in range(KB):
                    norm_high(2, b)
                norm_scale(2)
                for m in range(KB):
                    ahead(K_Q + m)

                def softmax(h):
                    act.wait_ge(sem["mx_ready"], h + 1)
                    if h >= 2:
                        act.wait_ge(sem["pt_done"], h - 1)
                    for c in range(2):
                        act.activation(pr[:, h % 2, c, :], bank[h % 2][:, c * TP:c * TP + TP], ACT.Exp, bias=nmx[:, h, c:c + 1],
                                       scale=1.0 / 16, accum_out=psm[:, h, c:c + 1]).then_inc(sem["p_ready"], 1)

                def probs_out(h):
                    act.wait_ge(sem["pt_done"], h + 1)
                    act.activation(prt[:, h % 2, :, :].rearrange("p m l -> p (m l)"), bank[2 + h % 2][:], ACT.Copy).then_inc(sem["prt_ready"], 1)

                def attended(h):
                    act.wait_ge(sem["pv_done"], h + 1)
                    for i in range(2):
                        act.activation(xn_hi[:, 2 * h + i, 0:TP], bank[4 + h % 2][:, i * TP:i * TP + TP], ACT.Copy).then_inc(sem["o_hi"], 1)

                softmax(0)
                for h in range(HEADS):
                    if h < HEADS - 1:
                        softmax(h + 1)
                    probs_out(h)
                    if h == 2:
                        act.wait_ge(sem["ss_mx"], 1)
                        act.activation(ps_s[:], bank[6][0:32, 0:TP], ACT.Exp, bias=m32[:, 1:2], scale=1.0 / 16,
                                       accum_out=m32[:, 2:3]).then_inc(sem["ss_p"], 1)
                    attended(h)
                act.wait_ge(sem["kv_used"], 2 * NS)
                act.activation(os_s[:], bank[6][0:32, 0:TP], ACT.Copy).then_inc(sem["ss_o"], 1)
                act.wait_ge(sem["ss_t3"], 1)
                for i in range(2):
                    act.activation(xn_hi[:, i:KB:2, TP:T], bank[7][:, 64 + 32 * i:96 + 32 * i].rearrange("p (b h) -> p h b", h=HEADS),
                                   ACT.Copy).then_inc(sem["o_hi"], 1)
                for m in range(KB):
                    ahead(K_O + m)
                    norm_square(3, m)
                for b in range(KB):
                    norm_high(3, b)

                ffn(1)
                layer_end(act, "act")

            chain[0] = 0
            for b in range(KB):
                act.activation(sq[:, b, :], x[:, b, :], ACT.Square).then_inc(sem["sq_ready"], 1)
            norm_scale(0)

        @block.vector
        def _(dve):
            chain = [0]

            def link(ins):
                chain[0] += 1
                ins.then_inc(sem["dve_chain"], 1)
                dve.wait_ge(sem["dve_chain"], chain[0])

            def over(ap, count):
                return ap.unsqueeze(2).to_broadcast([ap.shape[0], ap.shape[1], count])

            def each(ap, count):
                return ap.unsqueeze(1).to_broadcast([ap.shape[0], count, ap.shape[1]])

            def norm_low(n):
                for b in range(KB):
                    dve.wait_ge(sem["xn_hi"], KB * n + b + 1)
                    dve.scalar_tensor_tensor(xn_lo[:, b, :], x[:, b, :], pc(f"n{n + 1}", b, b + 1), xn_hi[:, b, :].bitcast(F32),
                                             ALU.mult, ALU.subtract).then_inc(sem["xn_lo"], 1)

            def ffn(f):
                k0 = (K_FFN1, K_FFN2)[f]
                norm_low((0, 3)[f])
                dve.wait_ge(sem["r_ready"], (1, 4)[f])
                with dve.Fori(0, 2) as half:
                    k = half * HALF_CH + k0
                    b = half * HALF + 2 * HALF * f

                    def low(j):
                        dve.wait_ge(sem["hhi_ready"], b + (j + 1))
                        dve.tensor_tensor(h_lo[:, j, :], h32[:, j % 2, :], h_hi[:, j, :].bitcast(F32), ALU.subtract).then_inc(sem["h_ready"], 1)

                    for j in range(HALF):
                        dve.wait_ge(sem["chunk_used"], k + (2 * j + 2))
                        dve.tensor_tensor(gbuf[:, j % 2, :], bank[2 * (j % 2)][:, 0:T], r_bc[:], ALU.mult).then_inc(sem["g_ready"], 1)
                        dve.tensor_tensor(ubuf[:, j % 2, :], bank[2 * (j % 2) + 1][:, 0:T], r_bc[:], ALU.mult).then_inc(sem["up_evac"], 1)
                        if j:
                            low(j - 1)
                        dve.wait_ge(sem["s_ready"], b + (j + 1))
                        dve.wait_ge(sem["up_evac"], b + (j + 1))
                        dve.tensor_tensor(h32[:, j % 2, :], sbuf_[:, j % 2, :], ubuf[:, j % 2, :], ALU.mult).then_inc(sem["h32_ready"], 1)
                    low(HALF - 1)
                    for m in range(KB):
                        if m < KB - 1:
                            dve.wait_ge(sem["down_done"], half * (KB - 1) + (2 * (KB - 1) * f + m + 1))
                        else:
                            dve.wait_ge(sem["chunk_used"], k + HALF_CH)
                        dve.scalar_tensor_tensor(x[:, m, :], bank[4 + m % 4][:, 0:T], 0.5, x[:, m, :], ALU.mult, ALU.add).then_inc(sem["x_done"], 1)

            dve.wait_ge(loaded, 48)
            with dve.Fori(0, depth):
                chain[0] = 0
                ffn(0)

                dve.memset(xp[:, :, 0:3], 0.0).then_inc(sem["conv_out_ready"], 1)
                dve.wait_ge(sem["st_in"], 48)
                dve.wait_ge(tables_in, 16)
                seg = xp[:, :, TP + 3:PADW].rearrange("p k (b j) -> p k b j", j=4)
                link(dve.tensor_copy(seg[:, :, :, 0:3], convld[:]))
                norm_low(1)
                dve.wait_ge(sem["ws_hi_ready"], 1)
                dve.tensor_tensor(ws_lo[:], pc("ws"), ws_hi[:].bitcast(F32), ALU.subtract).then_inc(sem["ws_ready"], 1)
                dve.wait_ge(sem["r_ready"], 2)

                def evac(n, *pairs, scale=None):
                    dve.wait_ge(sem["chunk_used"], K_WIN + n + 1)
                    for i, (dst, cols) in enumerate(pairs):
                        src = bank[n % 4][:, cols[0]:cols[1]]
                        if scale is None:
                            ins = dve.tensor_tensor(dst, src, r_bc[:, cols[0]:cols[1]], ALU.mult)
                        else:
                            ins = dve.scalar_tensor_tensor(dst, src, scale, r_bc[:, cols[0]:cols[1]], ALU.mult, ALU.mult)
                    ins.then_inc(sem["win_evac"], 1)

                for n in range(B_Z):
                    evac(n, (xp[:, n, 3:TP + 3], (0, TP)), (seg[:, n, :, 3], (TP, T)))
                    dve.wait_ge(sem["win_evac"], n + 1)
                    if n >= 2:
                        dve.wait_ge(sem["xs_ready"], n - 1)
                    w = lambda j: pc("cw", 4 * n + j, 4 * n + j + 1)
                    link(dve.tensor_scalar(cbuf[:, n % 2, :], xp[:, n, 0:288], w(0), pc("cb", n, n + 1), ALU.mult, ALU.add))
                    for j in range(1, 4):
                        ins = dve.scalar_tensor_tensor(cbuf[:, n % 2, :], xp[:, n, j:j + 288], w(j), cbuf[:, n % 2, :], ALU.mult, ALU.add)
                        if j < 3:
                            link(ins)
                    ins.then_inc(sem["conv_done"], 1)
                    if n == 0:
                        dve.wait_ge(sem["small_done"], 1)
                        dve.tensor_tensor(sm[:], bank[7][0:SM, 0:T], r_bc[0:SM, :], ALU.mult).then_inc(sem["small_evac"], 1)
                dve.tensor_copy(convst[:, :, 0, :], xp[:, :, TP:TP + 3])
                dve.tensor_copy(convst[:, :, 1:9, :], seg[:, :, :, 1:4]).then_inc(sem["conv_out_ready"], 1)
                for n in range(B_Z, B_GQ):
                    evac(n, (yg[:, n - B_Z, :], (0, T)))
                v8 = sm[0:8, :]
                dve.wait_ge(sem["small_evac"], 1)
                link(dve.tensor_scalar(v8, v8, pc("dtb", rows=slice(0, 8)), None, ALU.add))
                dve.scalar_tensor_tensor(sp[0][0:8, :], v8, -1.0, v8, ALU.mult, ALU.min).then_inc(sem["lp_dve"], 1)
                dve.wait_ge(sem["gate_done"], 1)
                link(dve.tensor_scalar(vg[:], bank[6][:, 0:T], pc("glab"), None, ALU.add))
                dve.scalar_tensor_tensor(ng[:], vg[:], -1.0, vg[:], ALU.mult, ALU.min).then_inc(sem["lp_dve"], 1)
                evac(B_GQ, (qkv[:, 0, :], (0, T)), scale=32.0 ** -0.5)
                evac(B_GK, (qkv[:, 1, :], (0, T)))
                evac(B_GV, (qkv[:, 2, :], (0, T)))
                for s, (e, u, w) in enumerate(((e8[:], dt8[:], sp[0][0:8, :]), (eg, ug, ng[:]))):
                    dve.wait_ge(sem["lp_act"], 1 + s)
                    link(dve.tensor_scalar(u, e, 1.0, None, ALU.add))
                    dve.scalar_tensor_tensor(w, u, 1.0, e, ALU.subtract, ALU.subtract).then_inc(sem["lp_dve"], 1)
                evac(B_GV + 1, (qkv[:, 3, :], (0, T)))
                evac(B_RQ, (qkv[:, 4, :], (0, T)))
                dve.wait_ge(sem["lp_act"], 3)
                dve.wait_ge(sem["lp_dve"], 4)
                link(dve.tensor_tensor(e8[:], e8[:], sp[0][0:8, :], ALU.subtract))
                link(dve.scalar_tensor_tensor(dt8[:], v8, 0.0, e8[:], ALU.max, ALU.add))
                dve.wait_ge(sem["z_ready"], 1)
                link(dve.tensor_scalar(la8[:], dt8[:], na8[:], -1.0, ALU.mult, ALU.mult))
                dve.tensor_copy(bsum[:, TP:T], la8[:, TP:T])
                dve.tensor_tensor_scan(bsum[:, 0:TP], cc("ones", 0, 1, rows=slice(0, 8)).to_broadcast([8, TP]), la8[:, 0:TP], 0.0,
                                       ALU.mult, ALU.add).then_inc(sem["bsum_ready"], 1)
                dve.wait_ge(sem["lp_act"], 4)
                link(dve.tensor_tensor(eg, eg, ng[:], ALU.subtract))
                link(dve.scalar_tensor_tensor(eg, vg[:], 0.0, eg, ALU.min, ALU.subtract))
                link(dve.tensor_scalar(eg, eg, 1.0 / 16, None, ALU.mult))
                dve.tensor_copy(glog[:, TP:T], eg[:, TP:T])
                link(dve.tensor_tensor_scan(glog[:, 0:TP], cc("ones", 0, 1).to_broadcast([P, TP]), eg[:, 0:TP], 0.0, ALU.mult, ALU.add))
                for n in range(B_RQ + 1, B_RV):
                    evac(n, (qkv[:, n - B_GQ, :], (0, T)))
                    if n in (B_RQ + 1, B_RK + 1):
                        a = n - B_GQ - 1
                        dve.wait_ge(sem["win_evac"], n + 1)
                        ab = qkv[:, a:a + 2, :]
                        dve.tensor_tensor(rp[0][:], ab, each(cc("cos"), 2), ALU.mult)
                        link(dve.tensor_tensor(rp[1][:], ab, each(cc("sin"), 2), ALU.mult))
                        dve.tensor_tensor(qkv[:, a, :], rp[0][:, 0, :], rp[1][:, 1, :], ALU.subtract)
                        link(dve.tensor_tensor(qkv[:, a + 1, :], rp[0][:, 1, :], rp[1][:, 0, :], ALU.add))
                dve.wait_ge(sem["mem_hi_ready"], 1)
                dve.tensor_tensor(mem_lo[:], mem_raw[:], mem_hi[:].bitcast(F32), ALU.subtract).then_inc(sem["mem_lo_ready"], 1)
                for n in range(B_RV, B_GG):
                    evac(n, (qkv[:, n - B_GQ, :], (0, T)))
                dve.wait_ge(sem["bs_done"], 1)
                dve.tensor_copy(bs[:].rearrange("p c h -> p (c h)"), bank[4][:, 0:16]).then_inc(sem["bs_ready"], 1)
                dve.wait_ge(sem["xs_ready"], 8)
                for i in range(4):
                    dve.wait_ge(sem["dtb_done"], i + 1)
                    dve.tensor_tensor(xdt[:, i, :], xc[:, i, :], bank[(5, 6, 7, 4)[i]][:, 0:T], ALU.mult).then_inc(sem["xdt_ready"], 1)


                def gate(n):
                    evac(n, (yg[:, n - B_GG + 4, :], (0, T)))

                gate(B_GG)
                for g in range(2):
                    dve.wait_ge(sem["g_done"], g + 1)
                    dve.tensor_tensor(gm[:, g, :], bank[4 + g][:, 0:384], cc("tri"), ALU.mult).then_inc(sem["gm_ready"], 1)

                def diffs(h):
                    dve.wait_ge(sem["bc_done"], h + 1)
                    dve.wait_ge(sem["bs_ready"], 1)
                    if h >= 2:
                        dve.wait_ge(sem["m_ready"], h - 1)
                    src, d = bank[6 + h % 2], dbuf[:, h % 2, :]
                    dve.tensor_scalar(d[:, 0:TP], src[:, 0:TP], bs[:, 0, h:h + 1], 0.0, ALU.subtract, ALU.min)
                    dve.tensor_scalar(d[:, TP:384], src[:, P:TP], bs[:, 1, h:h + 1], 0.0, ALU.subtract, ALU.min)
                    dve.tensor_copy(d[:, 384:392], src[:, TP:T]).then_inc(sem["d_ready"], 1)

                def decayed(h):
                    dve.wait_ge(sem["e_ready"], h + 1)
                    dve.wait_ge(sem["gm_ready"], 2)
                    if h >= 2:
                        dve.wait_ge(sem["y_done"], h - 1)
                    d, hc = dbuf[:, h % 2, :], slice(64 * h, 64 * h + 64)
                    dve.wait_ge(sem["xtok_ready"], 2)
                    for c in range(2):
                        dve.tensor_scalar(xtail[:, c, hc], xtok[:, c, hc], d[:, 255 + P * c:256 + P * c], None, ALU.mult)
                    dve.tensor_tensor(mbuf[:, h % 2, :], d[:, 0:384], gm[:, h // 4, :], ALU.mult).then_inc(sem["m_ready"], 1)

                def skip(i):
                    dve.wait_ge(sem["y_done"], 2 * i + 2)
                    dve.scalar_tensor_tensor(xc[:, i, 0:TP], xc[:, i, 0:TP], pc("dsk", i, i + 1), bank[4 + i % 2][:, 0:TP],
                                             ALU.mult, ALU.add).then_inc(sem["y_evac"], 1)

                gate(B_GG + 1)
                diffs(0)
                diffs(1)
                gate(B_GG + 2)
                decayed(0)
                diffs(2)
                for i in range(3):
                    decayed(2 * i + 1)
                    decayed(2 * i + 2)
                    diffs(2 * i + 3)
                    if i < 2:
                        diffs(2 * i + 4)
                    skip(i)
                    if i == 0:
                        gate(B_GG + 3)
                decayed(7)
                skip(3)
                dve.wait_ge(sem["st_ssd_in"], 16)
                for i in range(4):
                    b_col, s_i = xc[:, 4 + i // 2, TP:T], sst[:, i, :, :]
                    if i:
                        dve.wait_ge(sem["xb_done"], i)
                    dve.wait_ge(sem["xdt_ready"], 4)
                    dve.tensor_tensor(xe[:], over(xdt[:, i, TP:T], P), each(ident, NS), ALU.mult).then_inc(sem["xe_ready"], 1)
                    for q in range(2):
                        dve.tensor_tensor(s_i[:, :, 64 * q:64 * q + 64], s_i[:, :, 64 * q:64 * q + 64], over(dec[:, 2 * i + q, :], 64), ALU.mult)
                    dve.wait_ge(sem["xb_done"], i + 1)
                    for q in range(2):
                        ins = dve.tensor_tensor(tb[:, 4 * q:4 * q + 4, :], bank[6 + q][:].rearrange("p (b n) -> p b n", n=P),
                                                over(b_col[:, 4 * q:4 * q + 4], P), ALU.mult)
                    ins.then_inc(sem["xb_evac"], 1)
                    dve.wait_ge(sem["xb_evac"], i + 1)
                    dve.tensor_tensor(s_i, s_i, tb[:], ALU.add).then_inc(sem["sst_ready"], 1)
                dve.wait_ge(sem["ssdp_done"], 1)
                dve.wait_ge(sem["sst_ready"], 4)
                for l, span in enumerate(LEVELS):
                    pairs = glog[:, 0:TP].rearrange("p (n s) -> p n s", s=2 * span)
                    ref = pairs[:, :, span - 1:span].to_broadcast([P, TP // (2 * span), span])
                    out = ke[:, l, :].rearrange("p (n s) -> p n s", s=2 * span)
                    dve.tensor_tensor(out[:, :, 0:span], ref, pairs[:, :, 0:span], ALU.subtract)
                    dve.tensor_tensor(out[:, :, span:], pairs[:, :, span:], ref, ALU.subtract)
                dve.tensor_tensor(ke[:, 8, :], glog[:, TP - 1:TP].to_broadcast([P, TP]), glog[:, 0:TP], ALU.subtract).then_inc(sem["d9_ready"], 1)
                dve.wait_ge(sem["z_ready"], 2)
                dve.wait_ge(sem["y_evac"], 4)
                dve.wait_ge(sem["o_done"], 1)
                for i in range(4):
                    link(dve.scalar_tensor_tensor(xc[:, i, TP:T], xc[:, i, TP:T], pc("dsk", i, i + 1), bank[4][:, NS * i:NS * i + NS], ALU.mult, ALU.add))
                    dve.tensor_tensor(yg[:, i, :], yg[:, i, :], xc[:, i, :], ALU.mult).then_inc(sem["ssd_gated"], 1)

                dve.wait_ge(sem["e9_ready"], 1)
                link(dve.tensor_tensor(qe[:], ke[:, 0:8, :], each(qkv[:, 0, 0:TP], 8), ALU.mult))
                dve.tensor_tensor(ke[:], ke[:], each(qkv[:, 1, 0:TP], 9), ALU.mult).then_inc(sem["ke_ready"], 1)
                dve.wait_ge(sem["sg_done"], 2)
                rkt = gtmp[:].rearrange("p (a t) -> p a t", a=2)
                dve.tensor_tensor(rkt, qkv[:, 6:8, 0:TP], each(cc("rtail"), 2), ALU.mult).then_inc(sem["rkt_ready"], 1)
                dve.wait_ge(sem["sg_r"], 1)
                for i in range(4):
                    dve.scalar_tensor_tensor(yg[:, i, :], yg[:, i, :], pc("ssdw", i, i + 1), rn_s[:, i // 2, :], ALU.mult, ALU.mult).then_inc(sem["y_final"], 1)
                dve.wait_ge(sem["rktok_ready"], 1)

                def mixed_low(a, b):
                    for i in range(a, b):
                        dve.wait_ge(sem["y_hi"], i + 1)
                        dve.tensor_tensor(xn_lo[:, i, :], yg[:, i, :], xn_hi[:, i, :].bitcast(F32), ALU.subtract).then_inc(sem["y_lo"], 1)

                evacs = [0]
                for h in range(HEADS):
                    m3 = mg[:, h % 2, :]
                    acc = m3.rearrange("p (c n) -> p c n", n=P)[:, 0:3:2, :]
                    if h >= 2:
                        dve.wait_ge(sem["gy_done"], h - 1)
                    for r in range(4):
                        dve.wait_ge(sem["lv_done"], 5 * h + r + 1)
                        for l in range(2):
                            mask = each(cc("lmask", P * (2 * r + l), P * (2 * r + l) + P), 2)
                            src = bank[4 + (5 * h + r) % 2][:, 256 * l:256 * l + 256].rearrange("p (c n) -> p c n", n=P)
                            if r or l:
                                mask = each(cc("lmask", P * (2 * r + l), P * (2 * r + l) + P).bitcast(mybir.dt.int32), 2)
                            if r == 0 and l == 0:
                                link(dve.tensor_tensor(acc, src, mask, ALU.mult))
                            else:
                                ins = dve.copy_predicated(acc, mask, src)
                                if l:
                                    evacs[0] += 1
                                    ins.then_inc(sem["lv_evac"], 1)
                                    dve.wait_ge(sem["lv_evac"], evacs[0])
                                else:
                                    link(ins)
                    dve.wait_ge(sem["lv_done"], 5 * h + 5)
                    evacs[0] += 1
                    dve.tensor_copy(m3[:, P:TP], bank[4 + (5 * h + 4) % 2][:, 0:P]).then_inc(sem["lv_evac"], 1)
                    dve.wait_ge(sem["lv_evac"], evacs[0])
                    dve.sem_inc(sem["mg_ready"], 1)
                    if h == 1:
                        mixed_low(0, 4)
                dve.wait_ge(sem["gy_done"], 4)
                dve.tensor_copy(yb[:, 0:2, 0:TP], bank[6][:].rearrange("p (i t) -> p i t", i=2)).then_inc(sem["gy_evac"], 1)
                dve.wait_ge(sem["gs_done"], 1)
                for h in range(HEADS):
                    rows = slice(32 * h, 32 * h + 32)
                    dve.tensor_copy(sto[rows, 0, :], bank[7][rows, 64 * h:64 * h + 64]).then_inc(sem["gs_ready"], 1)

                def add_out(c):
                    outs, _ = OUT[c]
                    for u, m in enumerate(outs):
                        if u == len(outs) - 1:
                            dve.wait_ge(sem["chunk_used"], K_WOUT + c + 1)
                        else:
                            dve.wait_ge(sem["out_done"], OUT_AT[c] - c + u + 1)
                        dve.tensor_tensor(x[:, m, :], x[:, m, :], bank[(OUT_AT[c] + u) % 4][:, 0:T], ALU.add).then_inc(sem["x_done"], 1)

                for h in range(HEADS):
                    dve.wait_ge(sem["rsc_done"], h + 1)
                    if h < 2:
                        dve.wait_ge(sem["gy_done"], 4)
                    else:
                        dve.wait_ge(sem["ry_done"], h - 1)
                    dve.tensor_tensor(mg[:, h % 2, :], bank[4 + h % 2][:, 0:384], cc("decay", 384 * h, 384 * h + 384), ALU.mult).then_inc(sem["mr_ready"], 1)
                dve.wait_ge(sem["ry_done"], 4)
                dve.tensor_copy(yb[:, 2:4, 0:TP], bank[7][:].rearrange("p (i t) -> p i t", i=2)).then_inc(sem["ry_evac"], 1)
                dve.wait_ge(sem["rs_done"], 1)
                for j in range(2):
                    for h in range(HEADS):
                        rows = slice(32 * h, 32 * h + 32)
                        dve.tensor_copy(sto[rows, 1 + j, :], bank[6][rows, TP * j + 64 * h:TP * j + 64 * h + 64]).then_inc(sem["gs_ready"], 1)

                for kind in range(2):
                    v0 = (2, 8)[kind]
                    if kind:
                        dve.wait_ge(sem["vb_done"], 1)
                    for i in range(2):
                        dve.tensor_tensor(xg[:, i, :, :], over(qkv[:, v0 + i, TP:T], 64), each(cc("id64"), NS), ALU.mult).then_inc(sem["xg_ready"], 1)
                    if kind:
                        add_out(0)
                    for j in range(1 + kind):
                        s_j = gst[:] if kind == 0 else rst[:, j, :, :]
                        q_col, k_col = (qkv[:, 0, TP:T], qkv[:, 1, TP:T]) if kind == 0 else (qkv[:, 4 + j, TP:T], qkv[:, 6 + j, TP:T])
                        dve.tensor_tensor(qx[:, kind + j, :, :], over(q_col, 4), each(cc("hmask"), NS), ALU.mult).then_inc(sem["qx_ready"], 1)
                        if kind == 0:
                            dve.wait_ge(sem["gdec_ready"], 1)
                            link(dve.tensor_tensor(s_j, s_j, over(gdec[:], 64), ALU.mult))
                        else:
                            link(dve.tensor_scalar(s_j, s_j, cc("gamma"), None, ALU.mult))
                        dve.wait_ge(sem["vb_done"], kind + 1)
                        link(dve.tensor_tensor(tg[:], bank[4 + 2 * kind][:].rearrange("p (b n) -> p b n", n=64), over(k_col, 64), ALU.mult))
                        link(dve.scalar_tensor_tensor(s_j, tg[:], (1.0, 0.125)[kind], s_j, ALU.mult, ALU.add))
                        dve.sem_inc(sem["gst_ready"], 1)
                add_out(1)
                for kind in range(2):
                    dve.wait_ge(sem["go_done"], kind + 1)
                    for i in range(2):
                        dve.tensor_copy(yb[:, 2 * kind + i, TP:T], bank[5 if kind == 0 else 7][:, NS * i:NS * i + NS])\
                           .then_inc(sem[("gy_evac", "ry_evac")[kind]], 1)
                    if kind == 0:
                        dve.wait_ge(sem["gy_evac"], 3)
                        dve.sem_inc(sem["gy_evac"], 1)
                for i in range(2):
                    dve.wait_ge(sem["mu_done"], i + 1)
                    if i == 0:
                        dve.wait_ge(sem["ry_evac"], 3)
                    dve.tensor_tensor(yb[:, 2 + i, :], yb[:, 2 + i, :], bank[6 + i][:, 0:T], ALU.subtract).then_inc(sem["ry_evac"], 1)
                dve.wait_ge(sem["ry_evac"], 5)
                dve.sem_inc(sem["ry_evac"], 1)
                dve.wait_ge(sem["gg_ready"], 1)
                for kind in range(2):
                    if kind:
                        mixed_low(4, 6)
                        add_out(2)
                        add_out(3)
                    dve.wait_ge(sem["gms_r"], kind + 1)
                    for i in range(2):
                        y_i = yb[:, 2 * kind + i, :]
                        link(dve.scalar_tensor_tensor(y_i, y_i, pc(("glaw", "retw")[kind], i, i + 1), rn[:, 2 * kind + i, :], ALU.mult, ALU.mult))
                        dve.tensor_tensor(yg[:, 4 + 2 * kind + i, :], yg[:, 4 + 2 * kind + i, :], y_i, ALU.mult)\
                           .then_inc(sem["y_final"], 1)

                add_out(4)
                mixed_low(6, 8)
                def residual(k, m):
                    dve.wait_ge(sem["chunk_used"], k + m + 1)
                    dve.tensor_tensor(x[:, m, :], x[:, m, :], bank[m % 4][:, 0:T], ALU.add).then_inc(sem["x_done"], 1)

                for c in range(5, 8):
                    add_out(c)
                    if c == 5:
                        dve.wait_ge(sem["mix_out"], 64)
                        for i in range(2):
                            dve.memset(apart[i][:], 0.0).then_inc(sem["ss_zero"], 1)

                norm_low(2)
                dve.wait_ge(sem["r_ready"], 3)
                for m in range(KB):
                    dve.wait_ge(sem["chunk_used"], K_Q + m + 1)
                    dve.tensor_tensor(qt[:, m, :], bank[m % 4][:, 0:T], r_bc[:], ALU.mult).then_inc(sem["q_ready"], 1)

                dve.wait_ge(sem["q_ready"], KB)
                dve.wait_ge(sem["ss_zero"], 2)
                for i in range(2):
                    dve.tensor_copy(apart[i][:, 31:1024:32].rearrange("p (k b) -> p k b", b=NS), qt[:, 4 * i:4 * i + 4, TP:T]).then_inc(sem["ss_q"], 1)

                def head_max(h):
                    dve.wait_ge(sem["sc_done"], h + 1)
                    link(dve.tensor_reduce(mx[:, h, :], bank[h % 2][:].rearrange("p (c m) -> p c m", c=2), AX.X, ALU.max))
                    dve.tensor_scalar(nmx[:, h, :], mx[:, h, :], -1.0 / 16, None, ALU.mult).then_inc(sem["mx_ready"], 1)

                def head_norm(h):
                    dve.wait_ge(sem["p_ready"], 2 * h + 2)
                    link(dve.reciprocal(rsm[:, h, :], psm[:, h, :]))
                    for c in range(2):
                        dve.tensor_scalar(pr[:, h % 2, c, :], pr[:, h % 2, c, :], rsm[:, h, c:c + 1], None, ALU.mult).then_inc(sem["pn_ready"], 1)

                def head_low(h):
                    dve.wait_ge(sem["o_hi"], 2 * h + 2)
                    for i in range(2):
                        dve.tensor_tensor(xn_lo[:, 2 * h + i, 0:TP], bank[4 + h % 2][:, i * TP:i * TP + TP],
                                          xn_hi[:, 2 * h + i, 0:TP].bitcast(F32), ALU.subtract).then_inc(sem["o_lo"], 1)

                head_max(0)
                head_norm(0)
                for h in range(HEADS):
                    if h < HEADS - 1:
                        head_max(h + 1)
                        head_norm(h + 1)
                    if h == 2:
                        dve.wait_ge(sem["kv_used"], NS)
                        link(dve.tensor_reduce(m32[:, 0:1], bank[6][0:32, 0:TP], AX.X, ALU.max))
                        dve.tensor_scalar(m32[:, 1:2], m32[:, 0:1], -1.0 / 16, None, ALU.mult).then_inc(sem["ss_mx"], 1)
                    if h == 3:
                        dve.wait_ge(sem["ss_p"], 1)
                        link(dve.reciprocal(m32[:, 3:4], m32[:, 2:3]))
                        dve.tensor_scalar(ps_s[:], ps_s[:], m32[:, 3:4], None, ALU.mult).then_inc(sem["ss_pn"], 1)
                    head_low(h)
                dve.wait_ge(sem["ss_t2"], 1)
                dve.tensor_copy(apart[0][:, 31:1024:32], bank[7][:, 0:32])
                dve.tensor_copy(apart[1][:, 31:1024:32], bank[7][:, 32:64]).then_inc(sem["ss_pts"], 1)
                dve.wait_ge(sem["o_hi"], KB + 2)
                for i in range(2):
                    dve.tensor_tensor(xn_lo[:, i:KB:2, TP:T], bank[7][:, 64 + 32 * i:96 + 32 * i].rearrange("p (b h) -> p h b", h=HEADS),
                                      xn_hi[:, i:KB:2, TP:T].bitcast(F32), ALU.subtract).then_inc(sem["o_lo"], 1)
                for m in range(KB):
                    residual(K_O, m)

                ffn(1)
                layer_end(dve, "dve")

            dve.wait_ge(sem["r_ready"], 1)
            for b in range(KB):
                dve.scalar_tensor_tensor(yo[:, b, :], x[:, b, :], pc("n1", b, b + 1), r_bc[:], ALU.mult, ALU.mult).then_inc(sem["h_ready"], 1)

        @block.tensor
        def _(pe):
            def mm3(out, w, tile, moving, cols, start, stop, wide=False):
                a, b = tile
                hi, lo = moving
                pe.matmul(out, w[0][:, a:b], hi[:, cols[0]:cols[1]], start=start, stop=False)
                pe.matmul(out, w[0][:, a:b], lo[:, cols[0]:cols[1]], start=False, stop=False)
                return pe.matmul(out, w[1][:, a:b], hi[:, cols[0]:cols[1]], start=False, stop=stop)

            def parts(k):
                return w_hi[:, k % SPL, :], w_lo[:, k % SPL, :]

            def project(k, out, hi, lo, n=T, norm=None):
                pe.wait_ge(lo_ready, k + 1)
                for b in range(KB):
                    if norm is not None:
                        pe.wait_ge(sem["xn_lo"], KB * norm + b + 1)
                    ins = mm3(out[:, 0:n], parts(k), (P * b, P * b + P), (hi[:, b, :], lo[:, b, :]), (0, n), b == 0, b == KB - 1)
                ins.then_inc(sem["chunk_used"], 1)

            def token_sums(n):
                if n:
                    pe.wait_ge(sem["r_ready"], n)
                for b in range(KB):
                    pe.wait_ge(sem["sq_ready"], KB * n + b + 1)
                    ins = pe.matmul(SUMS[n][:, 0:T], ones, sq[:, b, :], start=b == 0, stop=b == KB - 1)
                ins.then_inc(sem["ss_ready"], 1)

            def ffn(f):
                k0 = (K_FFN1, K_FFN2)[f]
                token_sums((0, 3)[f])
                if f:
                    pe.wait_ge(sem["x_done"], X_DONE[3])
                with pe.Fori(0, 2) as half:
                    k = half * HALF_CH + k0
                    b = half * HALF + 2 * HALF * f
                    for j in range(HALF):
                        if j >= 2:
                            pe.wait_ge(sem["up_evac"], b + (j - 1))
                        for u in range(2):
                            pe.wait_ge(lo_ready, k + (2 * j + u + 1))
                            for i in range(KB):
                                if j == 0 and u == 0:
                                    pe.wait_ge(sem["xn_lo"], (0, 3 * KB)[f] + i + 1)
                                ins = mm3(bank[2 * (j % 2) + u][:, 0:T], parts(2 * j + u), (P * i, P * i + P),
                                          (xn_hi[:, i, :], xn_lo[:, i, :]), (0, T), i == 0, i == KB - 1)
                            ins.then_inc(sem["chunk_used"], 1)
                    for t in range(KB * HALF):
                        c, (m, i) = 2 * HALF + t // TILES, divmod(t, HALF)
                        if t % TILES == 0:
                            pe.wait_ge(lo_ready, k + (c + 1))
                        if m == 0:
                            pe.wait_ge(sem["h_ready"], b + (i + 1))
                        if m >= 4 and i == 0:
                            pe.wait_ge(sem["x_done"], half * KB + ((0, X_DONE[3])[f] + m - 3))
                        a = P * (t % TILES)
                        ins = mm3(bank[4 + m % 4][:, 0:T], parts(c), (a, a + P), (h_hi[:, i, :], h_lo[:, i, :]), (0, T), i == 0, i == HALF - 1)
                        if t % TILES == TILES - 1:
                            ins.then_inc(sem["chunk_used"], 1)
                        elif i == HALF - 1:
                            ins.then_inc(sem["down_done"], 1)

            pe.wait_ge(loaded, 48)
            with pe.Fori(0, depth):
                ffn(0)

                token_sums(1)
                pe.wait_ge(sem["x_done"], 16)

                def project_in(n):
                    if n == 3:
                        pe.wait_ge(sem["r_ready"], 2)
                    if n >= 4:
                        pe.wait_ge(sem["win_evac"], n - 3)
                    project(K_WIN + n, bank[n % 4], xn_hi, xn_lo, norm=1 if n == 0 else None)

                for n in range(B_GG):
                    project_in(n)
                    if n == 0:
                        pe.wait_ge(sem["ws_ready"], 1)
                        for b in range(KB):
                            ins = mm3(bank[7][:, 0:T], (ws_hi, ws_lo), (SM * b, SM * b + P), (xn_hi[:, b, :], xn_lo[:, b, :]), (0, T), b == 0, b == KB - 1)
                        ins.then_inc(sem["small_done"], 1)
                    if n == 2:
                        pe.wait_ge(sem["small_evac"], 1)
                        pe.wait_ge(sem["r_ready"], 2)
                        pe.matmul(bank[6][:, 0:T], pc("gwg", rows=slice(32, 48)), sm[32:48, :], start=True, stop=True).then_inc(sem["gate_done"], 1)

                def fill(k):
                    if k < K_MEMK:
                        project_in(k - K_WIN)
                        return
                    if k < K_MEMV:
                        m = k - K_MEMK
                        if m < 4:
                            pe.wait_ge(sem["win_evac"], 25 if m == 0 else N_WIN)
                        else:
                            pe.wait_ge(sem["mk_ready"], m - 3)
                        project(k, bank[m % 4], mem_hi, mem_lo, TP)
                        return
                    half, c = divmod(k - K_MEMV, 4)
                    if c == 0:
                        pe.wait_ge(sem["mk_ready"], (6, 8)[half])
                    pe.wait_ge(lo_ready, k + 1)
                    wh, wl = parts(k)
                    for u in range(2):
                        b = 2 * c + u
                        for m in range(2):
                            out, rows = bank[2 * half + m][:], slice(P * m, P * m + P)
                            cols = slice(512 * u, 512 * u + 512)
                            pe.matmul(out, mem_hi[:, b, rows], wh[:, cols], start=b == 0, stop=False)
                            pe.matmul(out, mem_lo[:, b, rows], wh[:, cols], start=False, stop=False)
                            ins = pe.matmul(out, mem_hi[:, b, rows], wl[:, cols], start=False, stop=b == KB - 1)
                    ins.then_inc(sem["chunk_used"], 1)

                def project_out(c):
                    k = K_WOUT + c
                    outs, ks = OUT[c]
                    pe.wait_ge(lo_ready, k + 1)
                    pe.wait_ge(sem["y_lo"], ks.stop)
                    for u in range(len(outs)):
                        j = OUT_AT[c] + u
                        if j < 4:
                            pe.wait_ge(sem["mv_ready"], 2 * (j // 2) + 2)
                        else:
                            pe.wait_ge(sem["x_done"], 16 + j - 3)
                        for i, b in enumerate(ks):
                            a = P * (len(ks) * u + i)
                            ins = mm3(bank[j % 4][:, 0:T], parts(k), (a, a + P), (xn_hi[:, b, :], xn_lo[:, b, :]), (0, T), i == 0, i == len(ks) - 1)
                        ins.then_inc(sem["chunk_used" if u == len(outs) - 1 else "out_done"], 1)

                pe.wait_ge(tables_in, 16)
                pe.wait_ge(sem["mem_lo_ready"], 1)
                pe.wait_ge(sem["bsum_ready"], 1)
                for c in range(2):
                    ins = pe.transpose(bank[4][:, 8 * c:8 * c + 8], bsum[:, P * c:P * c + P], cc("ident", 0, 8, rows=slice(0, 8)))
                ins.then_inc(sem["bs_done"], 1)
                for i in range(4):
                    if i == 3:
                        pe.wait_ge(sem["bs_ready"], 1)
                    if i == 1:
                        pe.wait_ge(sem["lp_dve"], 2)
                    for q in range(2):
                        sel = cc("ident", 2 * i + q, 2 * i + q + 1, rows=slice(0, 8)).to_broadcast([8, 64])
                        ins = pe.matmul(bank[(5, 6, 7, 4)[i]][64 * q:64 * q + 64, 0:T], sel, dt8[:], start=True, stop=True)
                    ins.then_inc(sem["dtb_done"], 1)
                fill(K_WIN + B_GG)
                pe.wait_ge(sem["xs_ready"], 8)
                pe.wait_ge(sem["xdt_ready"], 1)
                for g in range(2):
                    for c in range(2):
                        a = 256 * c + P * g
                        ins = pe.transpose(bank[5][:, a:a + P], xc[:, 4 + g, P * c:P * c + P], ident)
                ins.then_inc(sem["btok_done"], 1)
                pe.wait_ge(sem["xdt_ready"], 4)
                for c in range(2):
                    for i in range(4):
                        ins = pe.transpose(bank[6 + c][:, P * i:P * i + P], xdt[:, i, P * c:P * c + P], ident)
                    ins.then_inc(sem["xtok_done"], 1)
                for g in range(2):
                    if g == 1:
                        pe.wait_ge(sem["btok_ready"], 1)
                    for c in range(2):
                        ins = pe.matmul(bank[4 + g][:, 256 * c:256 + P * c], xc[:, 4 + g, P * c:P * c + P], xc[:, 6 + g, P * c:TP], start=True, stop=True)
                    ins.then_inc(sem["g_done"], 1)
                fill(K_WIN + B_GG + 1)

                def sums(h):
                    if h < 2:
                        pe.wait_ge(sem["xtok_ready"], h + 1)
                    else:
                        pe.wait_ge(sem["d_ready"], h - 1)
                    sel = cc("ident", h, h + 1, rows=slice(0, 8)).to_broadcast([8, P])
                    pe.matmul(bank[6 + h % 2][:, 0:T], sel, bsum[:], start=True, stop=True).then_inc(sem["bc_done"], 1)

                def head(out, lhs, matrix, done):
                    pe.matmul(out, lhs[0], matrix[:, 0:TP], start=True, stop=False, skip_group_check=True)
                    pe.matmul(out[:, P:TP], lhs[1], matrix[:, TP:384], start=False, stop=True, skip_group_check=True).then_inc(sem[done], 1)

                def ssd_head(h):
                    i = h // 2
                    pe.wait_ge(sem["m_ready"], h + 1)
                    if h % 2 == 0:
                        pe.wait_ge(sem["gm_ready"], 2)
                        if i >= 2:
                            pe.wait_ge(sem["y_evac"], i - 1)
                    q = 64 * (h % 2)
                    head(bank[4 + i % 2][q:q + 64, 0:TP], [xtok[:, c, 64 * h:64 * h + 64] for c in range(2)], mbuf[:, h % 2, :], "y_done")

                sums(0)
                sums(1)
                fill(K_WIN + B_GG + 2)
                for h in range(HEADS_S):
                    ssd_head(h)
                    if h + 2 < HEADS_S:
                        sums(h + 2)
                        if h % 2 == 0:
                            fill(K_WIN + B_GG + 3 + h // 2)
                pe.wait_ge(sem["m_ready"], 8)
                for g in range(2):
                    for c in range(2):
                        ins = pe.matmul(bank[6][:, 256 * g:256 * g + 256], btok[:, c, P * g:P * g + P], xtail[:, c, 256 * g:256 * g + 256],
                                        start=c == 0, stop=c == 1)
                ins.then_inc(sem["ssdp_done"], 1)
                fill(K_MEMK + 2)

                def spread(i):
                    pe.wait_ge(sem["xe_ready"], i + 1)
                    if i == 0:
                        pe.wait_ge(sem["ssdp_ready"], 1)
                    else:
                        pe.wait_ge(sem["xb_evac"], i)
                    for q in range(2):
                        ins = pe.matmul(bank[6 + q][:], ones, xe[:, 4 * q:4 * q + 4, :].rearrange("p b n -> p (b n)"), start=True, stop=True)
                    ins.then_inc(sem["xb_done"], 1)

                def sample_out(i):
                    pe.wait_ge(sem["sst_ready"], i + 1)
                    if i == 0:
                        pe.wait_ge(sem["y_evac"], 4)
                    for b in range(NS):
                        ins = pe.matmul(bank[4][:, NS * i + b:NS * i + b + 1], sst[:, i, b, :], xc[:, 6 + i // 2, TP + b:TP + b + 1], start=True, stop=True)
                    return ins

                spread(0)
                fill(K_MEMK + 3)
                spread(1)
                sample_out(0)
                fill(K_MEMK + 4)
                spread(2)
                sample_out(1)
                fill(K_MEMK + 5)
                spread(3)
                sample_out(2)
                fill(K_MEMK + 6)
                sample_out(3).then_inc(sem["o_done"], 1)
                fill(K_MEMK + 7)
                fill(K_MEMV)
                pe.wait_ge(sem["ssd_sq"], 1)
                pe.wait_ge(sem["xb_evac"], 4)
                for g in range(2):
                    for i in range(2):
                        ins = pe.matmul(bank[6 + g][:, 0:T], ones, sq_s[:, 2 * g + i, :], start=i == 0, stop=i == 1)
                    ins.then_inc(sem["sg_done"], 1)
                for kind in range(2):
                    for c in range(2):
                        for i in range(2):
                            a = 256 * c + P * i
                            ins = pe.transpose(bank[5 - kind][:, a:a + P], qkv[:, (2, 8)[kind] + i, P * c:P * c + P], ident)
                    ins.then_inc(sem["vt_done"], 1)
                fill(K_MEMV + 1)
                pe.wait_ge(sem["rkt_ready"], 1)
                pe.wait_ge(sem["vt_ready"], 2)
                for j in range(2):
                    for c in range(2):
                        a = 256 * j + P * c
                        ins = pe.transpose(bank[4][:, a:a + P], gtmp[:, 256 * j + P * c:256 * j + P * c + P], ident)
                ins.then_inc(sem["rkt_done"], 1)
                pe.wait_ge(sem["ke_ready"], 1)
                pe.wait_ge(sem["sg_r"], 1)
                for c in range(2):
                    ins = pe.transpose(bank[7][:, P * c:P * c + P], ke[:, 8, P * c:P * c + P], ident)
                ins.then_inc(sem["gkt_done"], 1)

                pe.wait_ge(sem["rktok_ready"], 1)
                n = 0
                for h in range(HEADS):
                    rows = slice(32 * h, 32 * h + 32)
                    for r in range(5):
                        out = bank[4 + n % 2]
                        if n >= 2:
                            pe.wait_ge(sem["lv_evac"], n - 1)
                        if r == 4:
                            ins = pe.matmul(out[:, 0:P], ke[rows, 0, 0:P], qe[rows, 0, P:TP], start=True, stop=True)
                        else:
                            for l in range(2):
                                for c in range(2):
                                    a, t = 256 * l + P * c, slice(P * c, P * c + P)
                                    if 2 * r + l < 7:
                                        kk, qq = ke[rows, 2 * r + l + 1, t], qe[rows, 2 * r + l + 1, t]
                                    else:
                                        kk, qq = qkv[rows, 1, t], qkv[rows, 0, t]
                                    ins = pe.matmul(out[:, a:a + P], kk, qq, start=True, stop=True)
                        ins.then_inc(sem["lv_done"], 1)
                        n += 1
                    if h == 0:
                        pe.wait_ge(sem["gkt_ready"], 1)
                        for c in range(2):
                            ins = pe.matmul(bank[7][:, 0:TP], gktok[:, c, :], gvtok[:, c, :], start=c == 0, stop=c == 1)
                        ins.then_inc(sem["gs_done"], 1)
                    fill(K_MEMV + 2 + h)
                    pe.wait_ge(sem["mg_ready"], h + 1)
                    q, i = 64 * (h % 2), h // 2
                    head(bank[6][q:q + 64, TP * i:TP * i + TP], [gvtok[:, c, 64 * h:64 * h + 64] for c in range(2)], mg[:, h % 2, :], "gy_done")

                def ret_scores(h):
                    rows = slice(32 * h, 32 * h + 32)
                    if h < 2:
                        pe.wait_ge(sem["lv_evac"], 20)
                    else:
                        pe.wait_ge(sem["mr_ready"], h - 1)
                    for c in range(2):
                        for j in range(2):
                            ins = pe.matmul(bank[4 + h % 2][:, 256 * c:256 + P * c], qkv[rows, 6 + j, P * c:P * c + P], qkv[rows, 4 + j, P * c:TP],
                                            start=j == 0, stop=j == 1)
                    ins.then_inc(sem["rsc_done"], 1)

                ret_scores(0)
                ret_scores(1)
                fill(K_MEMV + 6)
                pe.wait_ge(sem["gs_ready"], 4)
                for h in range(HEADS):
                    pe.wait_ge(sem["mr_ready"], h + 1)
                    q, i = 64 * (h % 2), h // 2
                    head(bank[7][q:q + 64, TP * i:TP * i + TP], [rvtok[:, c, 64 * h:64 * h + 64] for c in range(2)], mg[:, h % 2, :], "ry_done")
                    if h + 2 < HEADS:
                        ret_scores(h + 2)
                pe.wait_ge(sem["gy_evac"], 1)
                for j in range(2):
                    for c in range(2):
                        ins = pe.matmul(bank[6][:, TP * j:TP * j + TP], rktok[:, j, c, :], rvtok[:, c, :], start=c == 0, stop=c == 1)
                ins.then_inc(sem["rs_done"], 1)
                fill(K_MEMV + 7)

                for kind in range(2):
                    pe.wait_ge(sem["xg_ready"], 2 * kind + 2)
                    pe.wait_ge(sem["mr_ready"], 4)
                    if kind:
                        pe.wait_ge(sem["gs_ready"], 12)
                    for i in range(2):
                        ins = pe.matmul(bank[4 + 2 * kind][:], cc("vsel", P * i, P * i + P), xg[:, i, :, :].rearrange("p b n -> p (b n)"), start=i == 0, stop=i == 1)
                    ins.then_inc(sem["vb_done"], 1)
                    if kind == 0:
                        project_out(0)
                for kind in range(2):
                    out = bank[5 + 2 * kind]
                    if kind == 0:
                        pe.wait_ge(sem["gst_ready"], 1)
                        pe.wait_ge(sem["qx_ready"], 1)
                    if kind:
                        project_out(1)
                        pe.wait_ge(sem["gst_ready"], 3)
                        pe.wait_ge(sem["qx_ready"], 3)
                        pe.wait_ge(sem["ry_evac"], 1)
                    for b in range(NS):
                        for q in range(2):
                            for j in range(1 + kind):
                                s_b = gst[:, b, :] if kind == 0 else rst[:, j, b, :]
                                ins = pe.matmul(out[64 * q:64 * q + 64, b:b + NS + 1:NS], s_b, qx[:, kind + j, b, q:4:2], start=j == 0, stop=j == kind)
                    ins.then_inc(sem["go_done"], 1)
                pe.wait_ge(sem["ry_evac"], 3)
                for i in range(2):
                    pe.matmul(bank[6 + i][:, 0:T], cc("bones"), yb[:, 2 + i, :], start=True, stop=True).then_inc(sem["mu_done"], 1)
                pe.wait_ge(sem["gsq_ready"], 1)
                for i in range(2):
                    pe.matmul(bank[4 + i][:, 0:T], cc("bones"), sq4[:, i, :], start=True, stop=True).then_inc(sem["gms_done"], 1)
                project_out(2)
                pe.wait_ge(sem["gsq_ready"], 2)
                for i in range(2):
                    pe.wait_ge(sem["gms_r"], 1)
                    pe.matmul(bank[4 + i][:, 0:T], cc("bones"), sq4[:, 2 + i, :], start=True, stop=True).then_inc(sem["gms_done"], 1)

                for c in range(3, 8):
                    project_out(c)

                token_sums(2)
                for m in range(KB):
                    if m < 4:
                        pe.wait_ge(sem["x_done"], X_DONE[2])
                    else:
                        pe.wait_ge(sem["q_ready"], m - 3)
                    project(K_Q + m, bank[m % 4], xn_hi, xn_lo, norm=2 if m == 0 else None)
                pe.wait_ge(sem["q_ready"], KB)
                pe.wait_ge(sem["ktv_in"], 32)

                def scores(h):
                    if h >= 2:
                        pe.wait_ge(sem["p_ready"], 2 * h - 2)
                    for c in range(2):
                        for i in range(2):
                            ins = pe.matmul(bank[h % 2][:, TP * c:TP * c + TP], qt[:, 2 * h + i, P * c:P * c + P], kt[:, 2 * h + i, :], start=i == 0, stop=i == 1)
                    ins.then_inc(sem["sc_done"], 1)

                def probs(h):
                    pe.wait_ge(sem["pn_ready"], 2 * h + 2)
                    if h >= 2:
                        pe.wait_ge(sem["prt_ready"], h - 1)
                    for m in range(2):
                        for c in range(2):
                            a = TP * m + P * c
                            ins = pe.transpose(bank[2 + h % 2][:, a:a + P], pr[:, h % 2, c, P * m:P * m + P], ident)
                    ins.then_inc(sem["pt_done"], 1)

                def values(h):
                    pe.wait_ge(sem["prt_ready"], h + 1)
                    if h >= 2:
                        pe.wait_ge(sem["o_lo"], 2 * h - 2)
                    for i in range(2):
                        for m in range(2):
                            a = 256 * h + P * i
                            ins = pe.matmul(bank[4 + h % 2][:, TP * i:TP * i + TP], vt[:, m, a:a + P], prt[:, h % 2, m, :], start=m == 0, stop=m == 1)
                    ins.then_inc(sem["pv_done"], 1)

                def one_row(i, entry, row):
                    a = 32 * entry + 31 - row
                    return apart[i][:, a:a + 32]

                def sample_scores(b):
                    pe.wait_ge(sem[f"kv_in{b % 4}"], 16 * (b // 4 + 1))
                    if b == 0:
                        pe.wait_ge(sem["ss_q"], 2)
                    for d in range(KB):
                        ins = pe.matmul(bank[6][0:32, 0:TP], one_row(d // 4, NS * (d % 4) + b, HEADS * b + d // 2), kv[b % 4][:, TP * d:TP * d + TP],
                                        start=b == 0 and d == 0, stop=b == NS - 1 and d == KB - 1)
                    ins.then_inc(sem["kv_used"], 1)

                scores(0)
                scores(1)
                sample_scores(0)
                sample_scores(1)
                for h in range(HEADS):
                    if h == 2:
                        sample_scores(6)
                        sample_scores(7)
                    probs(h)
                    if h + 2 < HEADS:
                        scores(h + 2)
                        sample_scores(2 * h + 2)
                        sample_scores(2 * h + 3)
                    values(h)
                pe.wait_ge(sem["ss_pn"], 1)
                for m in range(2):
                    ins = pe.transpose(bank[7][:, 32 * m:32 * m + 32], ps_s[:, P * m:P * m + P], cc("ident", 0, 32, rows=slice(0, 32)))
                ins.then_inc(sem["ss_t2"], 1)
                pe.wait_ge(sem["ss_pts"], 1)
                for b in range(NS):
                    n = NS + b
                    pe.wait_ge(sem[f"kv_in{n % 4}"], 16 * (n // 4 + 1))
                    for h in range(HEADS):
                        for m in range(2):
                            r = HEADS * b + h
                            ins = pe.matmul(bank[6][0:32, 0:TP], one_row(m, r, r), kv[n % 4][:, D * m + TP * h:D * m + TP * h + TP],
                                            start=r == 0 and m == 0, stop=r == HEADS * NS - 1 and m == 1)
                    ins.then_inc(sem["kv_used"], 1)
                pe.wait_ge(sem["ss_o"], 1)
                for i in range(2):
                    ins = pe.transpose(bank[7][:, 64 + 32 * i:96 + 32 * i], os_s[:, P * i:P * i + P], cc("ident", 0, 32, rows=slice(0, 32)))
                ins.then_inc(sem["ss_t3"], 1)
                pe.wait_ge(sem["o_lo"], KB + 2)
                for m in range(KB):
                    if m >= 4:
                        pe.wait_ge(sem["x_done"], X_DONE[2] + m - 3)
                    project(K_O + m, bank[m % 4], xn_hi, xn_lo)

                ffn(1)
                layer_end(pe, "pe")

            token_sums(0)


PAST = 2048


def build_consts():
    c = np.zeros((P, NCST), np.float64)

    def put(name, a, rows=slice(0, P)):
        lo, hi = CST[name]
        c[rows, lo:hi] = a

    i = np.arange(P)
    put("ident", np.eye(P))
    put("ones", 1.0)
    upper = (i[:, None] <= i[None, :]).astype(np.float64)
    put("tri", np.concatenate([upper, np.ones((P, P)), upper], 1))
    pos = np.concatenate([np.arange(TP), np.full(NS, PAST)]).astype(np.float32)
    inv = (np.float32(10000.0) ** (-np.arange(32, dtype=np.float32) / np.float32(32))).astype(np.float32)
    ang = (pos[None, :] * inv[i % 32][:, None]).astype(np.float32).astype(np.float64)
    put("cos", np.cos(ang))
    put("sin", np.sin(ang))
    lg = np.log1p(-np.exp2(-5.0 - np.arange(HEADS)))
    dist = np.concatenate([np.arange(TP)[None, :] - i[:, None], i[None, :] - i[:, None]], 1)
    dec = [np.where(dist >= 0, np.exp(lg[h] * np.maximum(dist, 0)), 0.0) / 8 for h in range(HEADS)]
    put("decay", np.concatenate(dec, 1))
    head = i // 32
    put("rtail", np.exp(lg[head][:, None] * (TP - 1 - np.arange(TP))[None, :]) / 8)
    put("gamma", np.exp(lg[head])[:, None])
    masks = []
    for span in LEVELS[1:]:
        s, t = i[:, None], i[None, :]
        masks.append((s // (2 * span) == t // (2 * span)) & (s // span % 2 == 0) & (t // span % 2 == 1))
    masks.append(i[:, None] == i[None, :])
    put("lmask", np.concatenate(masks, 1))
    put("bones", (i[:, None] // 64 == i[None, :] // 64) / 64.0)
    put("vsel", np.concatenate([(2 * b + i[:, None] // 64 == head[None, :]) for b in range(2)], 1))
    put("hmask", head[:, None] == np.arange(4)[None, :])
    put("id64", i[:, None] % 64 == np.arange(64)[None, :])
    put("eps", EPS)
    return c.astype(np.float32)


def blocks(v):
    return np.swapaxes(v.reshape(v.shape[:-1] + (-1, P)), -1, -2)


def chunks_by_block(w):
    n, k, m = w.shape
    return w.reshape(n, k // P, P, m // P, P).transpose(0, 3, 2, 1, 4).reshape(n, m // P, P, k)


def lay_out(inputs):
    g = {k: np.asarray(v) for k, v in inputs.items()}
    depth = g["w_in"].shape[0]
    win = g["w_in"]
    z, xbc, dt, gq, gk, gv, gg, glr, rq, rk, rv, rg = np.split(
        win, np.cumsum([512, 1024, 8, 128, 128, 256, 256, 16, 256, 256, 256]), axis=2)

    def halves(w):
        return w.reshape(depth, D, HEADS, 2, 32).transpose(0, 1, 3, 2, 4).reshape(depth, D, 256)

    mixed = np.concatenate([xbc, z, gq, gk, gv, halves(rq), halves(rk), rv, gg, rg], axis=2)

    def ffn_chunks(up, down):
        u = chunks_by_block(up)
        gate, up_ = u[:, :2 * HALF], u[:, 2 * HALF:]
        pairs = np.stack([gate, up_], 2).reshape(depth, 2, 2 * HALF, P, CH)
        dn = down.reshape(depth, 2, HALF, P, KB, P).transpose(0, 1, 4, 2, 3, 5)
        dn = dn.reshape(depth, 2, HALF, TILES, P, P).transpose(0, 1, 2, 4, 3, 5).reshape(depth, 2, HALF, P, CH)
        return np.concatenate([pairs, dn], 2).reshape(depth, 2 * HALF_CH, P, CH)

    t = g["w_out"].reshape(depth, KB, P, KB, P).transpose(0, 3, 1, 2, 4)
    out = np.stack([t[:, outs.start:outs.stop, ks.start:ks.stop].reshape(depth, TILES, P, P).transpose(0, 2, 1, 3).reshape(depth, P, CH)
                    for outs, ks in OUT], 1)
    mv = g["xattn_w_v"].reshape(depth, 4, 2, P, 2, 512).transpose(0, 4, 1, 3, 2, 5).reshape(depth, 8, P, CH)
    w = np.concatenate([ffn_chunks(g["ffn1_w_up"], g["ffn1_w_down"]), chunks_by_block(mixed), chunks_by_block(g["xattn_w_k"]), mv,
                        out, chunks_by_block(g["xattn_w_q"]), chunks_by_block(g["xattn_w_o"]),
                        ffn_chunks(g["ffn2_w_up"], g["ffn2_w_down"])], 1)
    w = w.reshape(depth * NCH, P, CH)
    w = np.concatenate([w, w[:RAW]], 0)

    p = np.zeros((depth + 1, P, NPAR), np.float32)

    def put(name, a, rows=slice(0, P)):
        lo, hi = PAR[name]
        p[:depth, rows, lo:lo + a.shape[-1]] = a

    for name, key in (("n1", "norm_ffn1"), ("n2", "norm_mix"), ("n3", "norm_xattn"), ("n4", "norm_ffn2"), ("cb", "conv_b"),
                      ("ssdw", "ssd_norm_w"), ("glaw", "gla_norm_w"), ("retw", "ret_norm_w"), ("glab", "gla_b_gate")):
        put(name, blocks(g[key]))
    put("cw", g["conv_w"].reshape(depth, 4, 8, P).transpose(0, 3, 2, 1).reshape(depth, P, 32))
    small = np.zeros((depth, D, SM), np.float32)
    small[:, :, 0:8], small[:, :, 32:48] = dt, glr
    put("ws", small.reshape(depth, KB, P, SM).transpose(0, 2, 1, 3).reshape(depth, P, KB * SM))
    put("gwg", g["gla_w_gate"], slice(32, 48))
    put("dtb", g["dt_bias"][:, :, None], slice(0, 8))
    put("alog", g["a_log"][:, :, None], slice(0, 8))
    put("dsk", np.repeat(g["d_skip"].reshape(depth, 4, 2), 64, axis=2).transpose(0, 2, 1))
    lo, hi = PAR["n1"]
    p[depth, :, lo:hi] = blocks(g["final_norm_w"])

    tokens = np.concatenate([g["x_prompt"][0], g["x_sample"][:, 0]], 0)
    x = tokens.T.reshape(KB, P, T).transpose(1, 0, 2)
    mem = g["mem_prompt"][0].T.reshape(KB, P, TP).transpose(1, 0, 2)
    ck = g["cache_mem_k"].reshape(depth, NS, TP, KB, P).transpose(0, 1, 4, 3, 2).reshape(depth * NS, P, KB * TP)
    cv = g["cache_mem_v"].reshape(depth, NS, 2, P, D).transpose(0, 1, 3, 2, 4).reshape(depth * NS, P, 2 * D)
    ssd = g["state_ssd"].reshape(depth, NS, 4, 2, P, 64).transpose(0, 4, 2, 1, 3, 5).reshape(depth, P, 4 * NS * P)
    conv = g["state_ssd_conv"].reshape(depth, NS, 3, 8, P).transpose(0, 4, 3, 1, 2).reshape(depth, P, 8 * NS * 3)
    gla = g["state_gla"].reshape(depth, NS, P, 64).transpose(0, 2, 1, 3).reshape(depth, P, NS * 64)
    ret = g["state_ret"].reshape(depth, NS, HEADS, 2, 32, 64).transpose(0, 2, 4, 3, 1, 5).reshape(depth, P, 2 * NS * 64)
    return depth, [("wts", w), ("params", p), ("consts", build_consts()), ("x_in", x), ("mem_in", mem), ("ck", ck), ("cv", cv),
                   ("st_ssd", ssd), ("st_conv", conv), ("st_gla", gla), ("st_ret", ret)]


def kernel(**inputs):
    import concourse.bacc as bacc
    from concourse.bass_utils import run_bass_kernel_spmd as run

    depth, arrays = lay_out(inputs)
    nc = bacc.Bacc("TRN2", target_bir_lowering=False, num_devices=1)
    feed, args = {}, []
    for name, a in arrays:
        feed[f"in_{name}"] = np.ascontiguousarray(a)
        args.append(nc.dram_tensor(f"in_{name}", a.shape, F32, kind="ExternalInput").ap())
    outs = [("y", (P, KB, T)), ("conv", (depth, P, 8 * 9 * 3)), ("ssdp", (depth, P, 512)), ("grp", (depth, P, 192)),
            ("mk", (depth * KB, P, TP)), ("mv", (depth, P, 2, D)), ("ssds", (depth, P, 4 * NS * P)), ("glas", (depth, P, NS * 64)),
            ("rets", (depth, P, 2 * NS * 64))]
    for name, shape in outs:
        args.append(nc.dram_tensor(f"out_{name}", shape, F32, kind="ExternalOutput").ap())
    build(nc, depth, *args)
    r = run(nc, [feed], core_ids=[0]).results[0]
    o = {name: np.asarray(r[f"out_{name}"]).reshape(shape) for name, shape in outs}

    y = o["y"].transpose(2, 1, 0).reshape(T, D)
    conv = o["conv"].reshape(depth, P, 8, 9, 3).transpose(0, 3, 4, 2, 1).reshape(depth, 9, 3, 1024)
    ssd_p = o["ssdp"].reshape(depth, P, 8, 64).transpose(0, 2, 1, 3)[:, None]
    grp = o["grp"].reshape(depth, HEADS, 32, 3, 64)
    gla_p = grp[:, None, :, :, 0]
    ret_p = grp[:, :, :, 1:].transpose(0, 1, 3, 2, 4).reshape(depth, 1, HEADS, 64, 64)
    mk = o["mk"].reshape(depth, D, TP).transpose(0, 2, 1).reshape(depth, 1, TP, 4, 256)
    mv = o["mv"].transpose(0, 2, 1, 3).reshape(depth, 1, TP, 4, 256)
    ssd_s = o["ssds"].reshape(depth, P, 4, NS, 2, 64).transpose(0, 3, 2, 4, 1, 5).reshape(depth, NS, 8, P, 64)
    gla_s = o["glas"].reshape(depth, HEADS, 32, NS, 64).transpose(0, 3, 1, 2, 4)
    ret_s = o["rets"].reshape(depth, HEADS, 32, 2, NS, 64).transpose(0, 4, 1, 3, 2, 5).reshape(depth, NS, HEADS, 64, 64)
    c = np.ascontiguousarray
    return (c(y[None, :TP]), c(y[TP:, None]), c(ssd_p), c(conv[:, None, 0]), c(gla_p), c(ret_p), c(mk), c(mv),
            c(ssd_s), c(conv[:, 1:]), c(gla_s), c(ret_s))
```
